# Optimizing a Trainium2 kernel written in Bass

```python
import math
import jax, jax.numpy as jnp
from jax import lax
import numpy as np
import jax
import jax.numpy as jnp

D_MODEL = 1024
BATCH = 1
SEQ = 256
DEPTH = 1

PLE_DIM = 256
MOBA_HEADS = 8
MOBA_HEAD_DIM = D_MODEL // 16
MOBA_WIDTH = MOBA_HEADS * MOBA_HEAD_DIM
MOBA_BLOCK = 256
MOBA_TOPK = 3
MOBA_Q_CHUNK = 64
RET_HEADS = 4
RET_HEAD_DIM = D_MODEL // 8
RET_WIDTH = RET_HEADS * RET_HEAD_DIM
RET_CHUNK = 256
MIX_WIDTH = MOBA_WIDTH + RET_WIDTH
IN_PROJ_WIDTH = 3 * MOBA_WIDTH + 4 * RET_WIDTH
SEQ_PAD_MULTIPLE = 256
D_FF = 2816
CONV_WIDTH = 3
RMS_EPS = 1e-6
GN_EPS = 1e-5


def rmsnorm(x, g):
    xf = x.astype(jnp.float32)
    ms = jnp.mean(xf * xf, axis=-1, keepdims=True)
    return (xf * lax.rsqrt(ms + RMS_EPS)).astype(x.dtype) * g

def alibi_slopes(n_heads):
    return jnp.exp2(-8.0 * jnp.arange(1, n_heads + 1, dtype=jnp.float32) / n_heads)

def to_heads(t, n_heads, head_dim):
    b, s, _ = t.shape
    return t.reshape(b, s, n_heads, head_dim).transpose(0, 2, 1, 3)

def from_heads(t):
    b, h, s, d = t.shape
    return t.transpose(0, 2, 1, 3).reshape(b, s, h * d)

def moba_attention(q, k, v):
    B, H, S, Dh = q.shape
    nb = S // MOBA_BLOCK
    k_eff = min(MOBA_TOPK, nb)
    n_sel = k_eff * MOBA_BLOCK
    scale = Dh ** -0.5
    slopes = alibi_slopes(H)[:, None, None]
    kb = k.reshape(B, H, nb, MOBA_BLOCK, Dh)
    vb = v.reshape(B, H, nb, MOBA_BLOCK, Dh)
    kmean = jnp.mean(kb.astype(jnp.float32), axis=3).astype(k.dtype)
    kb_flat = kb.reshape(B * H * nb, MOBA_BLOCK, Dh)
    vb_flat = vb.reshape(B * H * nb, MOBA_BLOCK, Dh)
    head_base = (jnp.arange(B * H, dtype=jnp.int32) * nb).reshape(B, H, 1, 1)
    chunks_per_block = MOBA_BLOCK // MOBA_Q_CHUNK
    blk_pos = jnp.arange(MOBA_BLOCK, dtype=jnp.int32)
    blk_ids = jnp.arange(nb, dtype=jnp.int32)

    def one_chunk(c):
        start = c * MOBA_Q_CHUNK
        qc = lax.dynamic_slice_in_dim(q, start, MOBA_Q_CHUNK, axis=2)
        own = c // chunks_per_block
        q_pos = start + jnp.arange(MOBA_Q_CHUNK, dtype=jnp.int32)
        gate = jnp.einsum('bhqd,bhnd->bhqn', qc, kmean).astype(jnp.float32)
        gate = jnp.where(blk_ids < own, gate, -jnp.inf)
        gate_val, sel = lax.top_k(gate, k_eff)
        sel_valid = jnp.isfinite(gate_val)
        flat = head_base + sel
        k_sel = kb_flat[flat].reshape(B, H, MOBA_Q_CHUNK, n_sel, Dh)
        v_sel = vb_flat[flat].reshape(B, H, MOBA_Q_CHUNK, n_sel, Dh)
        s_sel = jnp.einsum('bhqd,bhqkd->bhqk', qc, k_sel).astype(jnp.float32) * scale
        key_pos_sel = (sel[..., None] * MOBA_BLOCK + blk_pos).reshape(B, H, MOBA_Q_CHUNK, n_sel)
        dist_sel = (q_pos[:, None] - key_pos_sel).astype(jnp.float32)
        s_sel = jnp.where(jnp.repeat(sel_valid, MOBA_BLOCK, axis=-1),
                          s_sel - slopes * dist_sel, -jnp.inf)
        k_own = lax.dynamic_index_in_dim(kb, own, axis=2, keepdims=False)
        v_own = lax.dynamic_index_in_dim(vb, own, axis=2, keepdims=False)
        s_own = jnp.einsum('bhqd,bhkd->bhqk', qc, k_own).astype(jnp.float32) * scale
        dist_own = q_pos[:, None] - (own * MOBA_BLOCK + blk_pos)[None, :]
        s_own = jnp.where(dist_own >= 0, s_own - slopes * dist_own.astype(jnp.float32), -jnp.inf)
        probs = jax.nn.softmax(jnp.concatenate([s_sel, s_own], axis=-1), axis=-1).astype(v.dtype)
        out = (jnp.einsum('bhqk,bhqkd->bhqd', probs[..., :n_sel], v_sel)
               + jnp.einsum('bhqk,bhkd->bhqd', probs[..., n_sel:], v_own))
        return out

    outs = lax.map(one_chunk, jnp.arange(S // MOBA_Q_CHUNK, dtype=jnp.int32))
    return jnp.moveaxis(outs, 0, 2).reshape(B, H, S, Dh)

def retention_chunkwise(q, k, v):
    B, H, S, Dh = q.shape
    C = RET_CHUNK
    nc = S // C
    gamma = 1.0 - jnp.exp2(-5.0 - jnp.arange(H, dtype=jnp.float32))
    log_g = jnp.log(gamma)
    idx = jnp.arange(C, dtype=jnp.float32)
    diff = idx[:, None] - idx[None, :]
    decay_intra = jnp.where(diff >= 0, jnp.exp(log_g[:, None, None] * jnp.maximum(diff, 0.0)), 0.0)
    q_decay = jnp.exp(log_g[:, None] * (idx + 1.0))[..., None]
    k_decay = jnp.exp(log_g[:, None] * (C - 1.0 - idx))[..., None]
    chunk_decay = jnp.exp(log_g * C)[:, None, None]
    k = k * (Dh ** -0.5)

    def chunks(t):
        return jnp.moveaxis(t.reshape(B, H, nc, C, Dh), 2, 0)

    def step(state, inp):
        qc, kc, vc = inp
        s = jnp.einsum('bhqd,bhkd->bhqk', qc, kc) * decay_intra
        inner = jnp.einsum('bhqk,bhkd->bhqd', s, vc)
        cross = jnp.einsum('bhqd,bhde->bhqe', qc * q_decay, state)
        new_state = chunk_decay * state + jnp.einsum('bhkd,bhke->bhde', kc * k_decay, vc)
        return new_state, inner + cross

    state0 = jnp.zeros((B, H, Dh, Dh), jnp.float32)
    _, outs = lax.scan(step, state0, (chunks(q), chunks(k), chunks(v)))
    return jnp.moveaxis(outs, 0, 2).reshape(B, H, S, Dh)

def head_groupnorm(o, g):
    mu = jnp.mean(o, axis=-1, keepdims=True)
    var = jnp.mean(jnp.square(o - mu), axis=-1, keepdims=True)
    return from_heads((o - mu) * lax.rsqrt(var + GN_EPS)) * g

def causal_dwconv(u, w, b):
    S = u.shape[1]
    up = jnp.pad(u, ((0, 0), (CONV_WIDTH - 1, 0), (0, 0)))
    out = b
    for j in range(CONV_WIDTH):
        out = out + w[j] * up[:, j:j + S]
    return out

def first_inputs(seed: int = 0) -> dict:
    key = jax.random.key(seed)
    ks = jax.random.split(key, 17)
    f32 = jnp.float32

    def nrm(k, shape, scale):
        return jax.random.normal(k, shape, f32) * scale

    def gain(k, shape):
        return 1.0 + 0.02 * jax.random.normal(k, shape, f32)

    return {
        "x": nrm(ks[0], (BATCH, SEQ, D_MODEL), 1.0),
        "p": nrm(ks[1], (DEPTH, BATCH, SEQ, PLE_DIM), 1.0),
        "attn_norm": gain(ks[2], (DEPTH, D_MODEL)),
        "w_in": nrm(ks[3], (DEPTH, D_MODEL, IN_PROJ_WIDTH), D_MODEL ** -0.5),
        "ret_norm": gain(ks[4], (DEPTH, RET_WIDTH)),
        "w_out": nrm(ks[5], (DEPTH, MIX_WIDTH, D_MODEL), MIX_WIDTH ** -0.5),
        "ffn_norm": gain(ks[6], (DEPTH, D_MODEL)),
        "w_up": nrm(ks[7], (DEPTH, D_MODEL, D_FF), D_MODEL ** -0.5),
        "w_gate": nrm(ks[8], (DEPTH, D_MODEL, D_FF), D_MODEL ** -0.5),
        "conv_w": nrm(ks[9], (DEPTH, CONV_WIDTH, D_FF), CONV_WIDTH ** -0.5),
        "conv_b": nrm(ks[10], (DEPTH, D_FF), 0.01),
        "w_down": nrm(ks[11], (DEPTH, D_FF, D_MODEL), D_FF ** -0.5),
        "ple_norm": gain(ks[12], (DEPTH, D_MODEL)),
        "w_ple": nrm(ks[13], (DEPTH, PLE_DIM, D_MODEL), PLE_DIM ** -0.5),
        "w_ple_gate": nrm(ks[14], (DEPTH, D_MODEL, D_MODEL), D_MODEL ** -0.5),
        "final_norm": gain(ks[15], (D_MODEL,)),
    }

def first_block(x, p, attn_norm, w_in, ret_norm, w_out, ffn_norm, w_up, w_gate, conv_w,
              conv_b, w_down, ple_norm, w_ple, w_ple_gate, final_norm):
    B, S, _ = x.shape
    S_pad = -(-S // SEQ_PAD_MULTIPLE) * SEQ_PAD_MULTIPLE
    split_points = [MOBA_WIDTH, 2 * MOBA_WIDTH, 3 * MOBA_WIDTH,
                    3 * MOBA_WIDTH + RET_WIDTH, 3 * MOBA_WIDTH + 2 * RET_WIDTH,
                    3 * MOBA_WIDTH + 3 * RET_WIDTH]
    for i in range(DEPTH):
        h = rmsnorm(x, attn_norm[i])
        proj = h @ w_in[i]
        proj = jnp.pad(proj, ((0, 0), (0, S_pad - S), (0, 0)))
        mq, mk, mv, rq, rk, rv, rg = jnp.split(proj, split_points, axis=-1)
        moba_out = from_heads(moba_attention(to_heads(mq, MOBA_HEADS, MOBA_HEAD_DIM),
                                             to_heads(mk, MOBA_HEADS, MOBA_HEAD_DIM),
                                             to_heads(mv, MOBA_HEADS, MOBA_HEAD_DIM)))
        ret = retention_chunkwise(to_heads(rq, RET_HEADS, RET_HEAD_DIM),
                                  to_heads(rk, RET_HEADS, RET_HEAD_DIM),
                                  to_heads(rv, RET_HEADS, RET_HEAD_DIM))
        ret_out = (head_groupnorm(ret, ret_norm[i]) * jax.nn.silu(rg)).astype(x.dtype)
        mix = jnp.concatenate([moba_out, ret_out], axis=-1)[:, :S]
        x = x + mix @ w_out[i]
        h = rmsnorm(x, ffn_norm[i])
        u = causal_dwconv(h @ w_up[i], conv_w[i], conv_b[i])
        x = x + (jax.nn.gelu(u) * (h @ w_gate[i])) @ w_down[i]
        g = jax.nn.sigmoid(rmsnorm(x, ple_norm[i]) @ w_ple_gate[i])
        x = x + (p[i] @ w_ple[i]) * g
    return rmsnorm(x, final_norm)


CHUNK = 64
EPS = 1e-6
ROPE_THETA = 10000.0
A_HEADS = 8
A_DK = 64
A_DV = 64
CONV_K = 4
B_HEADS = 8
B_KV_HEADS = 2
B_HD = 64
IDX_HEADS = 8
IDX_HD = 64
TOPK_MAX = 256
N_GROUPS = 4
EXPERTS_PER_GROUP = 4
N_EXPERTS = N_GROUPS * EXPERTS_PER_GROUP
TOPK_IN_GROUP = 2
D_EXPERT = 256

A_QK_W = A_HEADS * A_DK
A_V_W = A_HEADS * A_DV
B_Q_W = B_HEADS * B_HD
B_KV_W = B_KV_HEADS * B_HD
CONV_W = 2 * A_QK_W + A_V_W
IN_SPLITS = (
    ("a_q", A_QK_W), ("a_k", A_QK_W), ("a_v", A_V_W), ("a_z", A_V_W),
    ("a_beta", A_HEADS), ("a_alpha", A_HEADS),
    ("b_q", B_Q_W), ("b_k", B_KV_W), ("b_v", B_KV_W),
    ("i_q", IDX_HEADS * IDX_HD), ("i_k", IDX_HD), ("i_w", IDX_HEADS),
    ("gate_a", D_MODEL), ("gate_b", D_MODEL),
)
D_IN = sum(n for _, n in IN_SPLITS)


def rmsnorm_2(x, g):
    xf = x.astype(jnp.float32)
    y = xf * lax.rsqrt(jnp.mean(xf * xf, axis=-1, keepdims=True) + EPS)
    return (y * g.astype(jnp.float32)).astype(x.dtype)

def l2norm(x):
    xf = x.astype(jnp.float32)
    return xf * lax.rsqrt(jnp.sum(xf * xf, axis=-1, keepdims=True) + EPS)

def split_cols(z):
    parts, off = {}, 0
    for name, n in IN_SPLITS:
        parts[name] = z[..., off:off + n]
        off += n
    return parts

def rope(x, pos):
    half = x.shape[-1] // 2
    inv = ROPE_THETA ** (-jnp.arange(half, dtype=jnp.float32) / half)
    ang = pos.astype(jnp.float32)[..., None] * inv
    cos = jnp.cos(ang)[:, :, None, :]
    sin = jnp.sin(ang)[:, :, None, :]
    xf = x.astype(jnp.float32)
    x1, x2 = xf[..., :half], xf[..., half:]
    return jnp.concatenate([x1 * cos - x2 * sin, x2 * cos + x1 * sin], axis=-1).astype(x.dtype)

def causal_dwconv_2(x, w):
    c = x.shape[-1]
    return lax.conv_general_dilated(
        x, w[:, None, :].astype(x.dtype), window_strides=(1,), padding=[(CONV_K - 1, 0)],
        dimension_numbers=("NWC", "WIO", "NWC"), feature_group_count=c)

def gated_delta_rule(q, k, v, g, beta):
    b, s, h, dk = q.shape
    dv = v.shape[-1]
    n = s // CHUNK

    def chunks(t):
        return jnp.moveaxis(t.reshape((b, n, CHUNK, h) + t.shape[3:]), 3, 1)

    qc, kc, vc, gc, bc = chunks(q), chunks(k), chunks(v), chunks(g), chunks(beta)
    G = jnp.cumsum(gc, axis=-1)
    idx = jnp.arange(CHUNK)
    incl = idx[:, None] >= idx[None, :]
    strict = idx[:, None] > idx[None, :]
    decay = jnp.exp(jnp.where(incl, G[..., :, None] - G[..., None, :], -jnp.inf))
    kk = jnp.einsum("bhnid,bhnjd->bhnij", kc, kc)
    a_mat = jnp.where(strict, bc[..., :, None] * kk * decay, 0.0) + jnp.eye(CHUNK, dtype=jnp.float32)
    rhs = jnp.concatenate([vc * bc[..., None], kc * (bc * jnp.exp(G))[..., None]], axis=-1)
    sol = lax.linalg.triangular_solve(a_mat, rhs, left_side=True, lower=True, unit_diagonal=True)
    u, w = sol[..., :dv], sol[..., dv:]
    qk = jnp.einsum("bhnid,bhnjd->bhnij", qc, kc) * decay
    q_dec = qc * jnp.exp(G)[..., None]
    k_dec = kc * jnp.exp(G[..., -1:] - G)[..., None]
    g_last = jnp.exp(G[..., -1])

    def step(state, xs):
        u_n, w_n, q_n, qk_n, k_n, gl_n = xs
        v_new = u_n - jnp.einsum("bhck,bhkv->bhcv", w_n, state)
        o_n = jnp.einsum("bhck,bhkv->bhcv", q_n, state) + jnp.einsum("bhij,bhjv->bhiv", qk_n, v_new)
        state = state * gl_n[..., None, None] + jnp.einsum("bhck,bhcv->bhkv", k_n, v_new)
        return state, o_n

    xs = tuple(jnp.moveaxis(t, 2, 0) for t in (u, w, q_dec, qk, k_dec, g_last))
    s0 = jnp.zeros((b, h, dk, dv), jnp.float32)
    _, o = lax.scan(step, s0, xs)
    return jnp.transpose(o, (1, 0, 3, 2, 4)).reshape(b, s, h, dv)

def dsa_attention(q, k, v, qi, ki, wi):
    b, s, hq, d = q.shape
    hk = k.shape[2]
    grp = hq // hk
    n = s // CHUNK
    topk = min(TOPK_MAX, s // 4)
    kf = k.reshape(b, s, hk * d)
    vf = v.reshape(b, s, hk * d)
    kif = ki.astype(jnp.float32)
    key_pos = jnp.arange(s)
    gather = jax.vmap(lambda table, ids: table[ids])

    def to_blocks(t):
        return jnp.moveaxis(t.reshape((b, n, CHUNK) + t.shape[2:]), 1, 0)

    def block(args):
        q_b, qi_b, wi_b, blk = args
        limit = (blk + 1) * CHUNK
        rel = jax.nn.relu(jnp.einsum("bthd,bsd->bths", qi_b.astype(jnp.float32), kif))
        score = jnp.einsum("bth,bths->bts", wi_b.astype(jnp.float32), rel)
        score = jnp.where(key_pos < limit, score, -jnp.inf)
        _, sel = lax.top_k(score, topk)
        valid = sel < limit
        ks = gather(kf, sel).reshape(b, CHUNK, topk, hk, d)
        vs = gather(vf, sel).reshape(b, CHUNK, topk, hk, d)
        qg = q_b.reshape(b, CHUNK, hk, grp, d)
        logits = jnp.einsum("btkgd,btjkd->btkgj", qg, ks).astype(jnp.float32) * (d ** -0.5)
        logits = jnp.where(valid[:, :, None, None, :], logits, -jnp.inf)
        p = jax.nn.softmax(logits, axis=-1).astype(v.dtype)
        o = jnp.einsum("btkgj,btjkd->btkgd", p, vs)
        return o.reshape(b, CHUNK, hq * d)

    out = lax.map(block, (to_blocks(q), to_blocks(qi), to_blocks(wi), jnp.arange(n)))
    return jnp.moveaxis(out, 0, 1).reshape(b, s, hq * d)

def hier_moe(h, w_rg, b_rg, w_re, b_re, w1, w3, w2):
    bsz, s, d = h.shape
    xt = h.reshape(-1, d)
    glog = (xt @ w_rg + b_rg).astype(jnp.float32)
    gp = jax.nn.softmax(glog, axis=-1)
    gsel = jnp.argmax(glog, axis=-1)
    ggate = jnp.take_along_axis(gp, gsel[:, None], axis=-1)
    elog = (xt @ w_re + b_re).astype(jnp.float32).reshape(-1, N_GROUPS, EXPERTS_PER_GROUP)
    elog_g = jnp.take_along_axis(elog, gsel[:, None, None], axis=1)[:, 0]
    ep = jax.nn.softmax(elog_g, axis=-1)
    top_p, top_i = lax.top_k(ep, TOPK_IN_GROUP)
    top_p = top_p / jnp.sum(top_p, axis=-1, keepdims=True)
    wts = ggate * top_p
    eid = gsel[:, None] * EXPERTS_PER_GROUP + top_i
    comb = jnp.sum(jax.nn.one_hot(eid, N_EXPERTS, dtype=jnp.float32) * wts[..., None], axis=1)
    act = jax.nn.silu(jnp.einsum("nd,edf->nef", xt, w1)) * jnp.einsum("nd,edf->nef", xt, w3)
    act = act * comb[:, :, None].astype(act.dtype)
    y = jnp.einsum("nef,efd->nd", act, w2)
    return y.reshape(bsz, s, d)

def second_inputs(seed: int = 0) -> dict:
    key = jax.random.key(seed)
    ks = jax.random.split(key, 24)
    f32 = jnp.float32

    def nrm(k, shape, fan):
        return jax.random.normal(k, shape, f32) * (fan ** -0.5)

    def gain(k, shape):
        return 1.0 + 0.02 * jax.random.normal(k, shape, f32)

    x = jax.random.normal(ks[0], (BATCH, SEQ, D_MODEL), f32)
    offs = jax.random.randint(ks[1], (BATCH, 1), 0, 64) * CHUNK
    positions = (offs + jnp.arange(SEQ, dtype=jnp.int32)[None, :]).astype(jnp.int32)
    norm1_g = gain(ks[2], (DEPTH, D_MODEL))
    w_in = nrm(ks[3], (DEPTH, D_MODEL, D_IN), D_MODEL)
    b_gate = 0.02 * jax.random.normal(ks[4], (DEPTH, 2 * D_MODEL), f32)
    conv_w = nrm(ks[5], (DEPTH, CONV_K, CONV_W), CONV_K)
    a_log = jnp.log(jax.random.uniform(ks[6], (DEPTH, A_HEADS), f32, 1.0, 16.0))
    dt = jnp.exp(jax.random.uniform(ks[7], (DEPTH, A_HEADS), f32, math.log(1e-3), math.log(1e-1)))
    dt_bias = dt + jnp.log(-jnp.expm1(-dt))
    a_norm_g = gain(ks[8], (DEPTH, A_DV))
    w_proj_a = nrm(ks[9], (DEPTH, A_V_W, D_MODEL), A_V_W)
    w_proj_b = nrm(ks[10], (DEPTH, B_Q_W, D_MODEL), B_Q_W)
    w_out = nrm(ks[11], (DEPTH, D_MODEL, D_MODEL), D_MODEL)
    norm2_g = gain(ks[12], (DEPTH, D_MODEL))
    w_router_group = nrm(ks[13], (DEPTH, D_MODEL, N_GROUPS), D_MODEL)
    b_router_group = 0.01 * jax.random.normal(ks[14], (DEPTH, N_GROUPS), f32)
    w_router_expert = nrm(ks[15], (DEPTH, D_MODEL, N_EXPERTS), D_MODEL)
    b_router_expert = 0.01 * jax.random.normal(ks[16], (DEPTH, N_EXPERTS), f32)
    w_exp_gate = nrm(ks[17], (DEPTH, N_EXPERTS, D_MODEL, D_EXPERT), D_MODEL)
    w_exp_up = nrm(ks[18], (DEPTH, N_EXPERTS, D_MODEL, D_EXPERT), D_MODEL)
    w_exp_down = nrm(ks[19], (DEPTH, N_EXPERTS, D_EXPERT, D_MODEL), D_EXPERT)
    final_norm_g = gain(ks[20], (D_MODEL,))
    return {
        "x": x, "positions": positions, "norm1_g": norm1_g, "w_in": w_in, "b_gate": b_gate,
        "conv_w": conv_w, "a_log": a_log, "dt_bias": dt_bias, "a_norm_g": a_norm_g,
        "w_proj_a": w_proj_a, "w_proj_b": w_proj_b, "w_out": w_out, "norm2_g": norm2_g,
        "w_router_group": w_router_group, "b_router_group": b_router_group,
        "w_router_expert": w_router_expert, "b_router_expert": b_router_expert,
        "w_exp_gate": w_exp_gate, "w_exp_up": w_exp_up, "w_exp_down": w_exp_down,
        "final_norm_g": final_norm_g,
    }

def second_block(x, positions, norm1_g, w_in, b_gate, conv_w, a_log, dt_bias, a_norm_g,
              w_proj_a, w_proj_b, w_out, norm2_g, w_router_group, b_router_group,
              w_router_expert, b_router_expert, w_exp_gate, w_exp_up, w_exp_down, final_norm_g):
    b, s, _ = x.shape
    for l in range(DEPTH):
        h = rmsnorm_2(x, norm1_g[l])
        parts = split_cols(h @ w_in[l])

        qkv = jnp.concatenate([parts["a_q"], parts["a_k"], parts["a_v"]], axis=-1)
        qkv = jax.nn.silu(causal_dwconv_2(qkv, conv_w[l]))
        aq = l2norm(qkv[..., :A_QK_W].reshape(b, s, A_HEADS, A_DK)) * (A_DK ** -0.5)
        ak = l2norm(qkv[..., A_QK_W:2 * A_QK_W].reshape(b, s, A_HEADS, A_DK))
        av = qkv[..., 2 * A_QK_W:].reshape(b, s, A_HEADS, A_DV).astype(jnp.float32)
        beta = jax.nn.sigmoid(parts["a_beta"].astype(jnp.float32))
        g = -jnp.exp(a_log[l].astype(jnp.float32)) * jax.nn.softplus(
            parts["a_alpha"].astype(jnp.float32) + dt_bias[l].astype(jnp.float32))
        o_a = gated_delta_rule(aq, ak, av, g, beta)
        o_a = rmsnorm_2(o_a, a_norm_g[l]) * jax.nn.silu(
            parts["a_z"].reshape(b, s, A_HEADS, A_DV).astype(jnp.float32))
        o_a = o_a.reshape(b, s, A_V_W).astype(x.dtype)

        bq = rope(parts["b_q"].reshape(b, s, B_HEADS, B_HD), positions)
        bk = rope(parts["b_k"].reshape(b, s, B_KV_HEADS, B_HD), positions)
        bv = parts["b_v"].reshape(b, s, B_KV_HEADS, B_HD)
        iq = rope(parts["i_q"].reshape(b, s, IDX_HEADS, IDX_HD), positions)
        ik = rope(parts["i_k"][:, :, None, :], positions)[:, :, 0, :]
        iw = parts["i_w"] * ((IDX_HEADS ** -0.5) * (IDX_HD ** -0.5))
        o_b = dsa_attention(bq, bk, bv, iq, ik, iw)

        gate_a = jax.nn.sigmoid(parts["gate_a"] + b_gate[l][:D_MODEL])
        gate_b = jax.nn.sigmoid(parts["gate_b"] + b_gate[l][D_MODEL:])
        merged = gate_a * (o_a @ w_proj_a[l]) + gate_b * (o_b @ w_proj_b[l])
        x = x + merged @ w_out[l]

        x = x + hier_moe(rmsnorm_2(x, norm2_g[l]), w_router_group[l], b_router_group[l],
                         w_router_expert[l], b_router_expert[l],
                         w_exp_gate[l], w_exp_up[l], w_exp_down[l])
    return rmsnorm_2(x, final_norm_g)


def setup_inputs(seed=0):
    out = dict(first_inputs(seed))
    for name, value in second_inputs(seed + 1).items():
        if name != "x":
            out[name + "_2"] = value
    return out


def reference(
    x, p, attn_norm, w_in, ret_norm, w_out, ffn_norm, w_up, w_gate, conv_w, conv_b, w_down,
    ple_norm, w_ple, w_ple_gate, final_norm, positions_2, norm1_g_2, w_in_2, b_gate_2, conv_w_2,
    a_log_2, dt_bias_2, a_norm_g_2, w_proj_a_2, w_proj_b_2, w_out_2, norm2_g_2,
    w_router_group_2, b_router_group_2, w_router_expert_2, b_router_expert_2, w_exp_gate_2,
    w_exp_up_2, w_exp_down_2, final_norm_g_2,
):
    x = first_block(
        x, p, attn_norm, w_in, ret_norm, w_out, ffn_norm, w_up, w_gate, conv_w, conv_b, w_down,
        ple_norm, w_ple, w_ple_gate, final_norm,
    )
    return second_block(
        x, positions_2, norm1_g_2, w_in_2, b_gate_2, conv_w_2, a_log_2, dt_bias_2, a_norm_g_2,
        w_proj_a_2, w_proj_b_2, w_out_2, norm2_g_2, w_router_group_2, b_router_group_2,
        w_router_expert_2, b_router_expert_2, w_exp_gate_2, w_exp_up_2, w_exp_down_2,
        final_norm_g_2,
    )


_drawn_inputs = setup_inputs


def setup_inputs(seed=0):
    import zlib

    import numpy as np

    out = dict(_drawn_inputs(seed))
    spreads = {}
    factors = {'ret_norm': 3.156,
     'conv_b': 2.995,
     'ple_norm': 20.898,
     'b_gate_2': 8.0,
     'a_norm_g_2': 13.444,
     'b_router_group_2': 40.295,
     'b_router_expert_2': 20.314,
     'final_norm_g_2': 8.005,
     'norm2_g_2': 3.646}
    for name, (base, spread) in spreads.items():
        noise = np.random.default_rng([zlib.crc32(name.encode()), seed]).standard_normal(out[name].shape)
        drawn = base * np.exp(spread * noise) if base else spread * noise
        out[name] = jnp.asarray(drawn.astype(out[name].dtype))
    for name, factor in factors.items():
        out[name] = (out[name] * factor).astype(out[name].dtype)
    return out
```

```python
from contextlib import ExitStack

import numpy as np

import concourse.bass as bass
from concourse import mybir
from concourse.alu_op_type import AluOpType as ALU

F32 = mybir.dt.float32
F32R = mybir.dt.float32r
I32 = mybir.dt.int32
ACT = mybir.ActivationFunctionType
AX_X = mybir.AxisListType.X

P = 128
S = 256
NT = S // P
D = 1024
KD = D // P
HD = 64
HEADS = 8
RET_HEADS = 4
D_FF = 2816
FFN_TILES = D_FF // P
PLE_CHUNKS = 256 // P
CHUNK = 64
N_EXPERTS = 16
TOPK = 64
QUARTER = 1024
RING = 6
LEAD = 4
RMS_EPS = 1e-6
GN_EPS = 1e-5
BIG = 1e30
N_CONSTANT_LOADS = 7
ARENA = 18688
RSQRT_SEED = 0x5F3759DF
ROUND = 1.5 * 2.0 ** 23
TWO_PI = (201 / 32, 1015 / 2 ** 19, 2 * np.pi - 201 / 32 - 1015 / 2 ** 19)

(B_MQ, B_MK, B_MV, B_RQ, B_RK, B_RV, B_RG, B_WOUT) = (0, 1, 2, 3, 4, 5, 6, 7)
B_FFN = 9
FFN_STEPS = FFN_TILES // 4
B_FFN_LAST = B_FFN + 3 * FFN_STEPS
B_PLE_DOWN = B_FFN_LAST + 1
B_PLE_GATE = B_PLE_DOWN + 1
B_IQ = B_PLE_GATE + 2
B_KV = B_IQ + 1
B_BQ = B_KV + 1
B_AQ = B_BQ + 1
B_AZ = B_AQ + 3
B_GATES = B_AZ + 1
B_PROJ = B_GATES + 4
B_WOUT2 = B_PROJ + 2
B_MOE = B_WOUT2 + 2
MOE_STEPS = N_EXPERTS // 2
N_BLOCKS = B_MOE + 3 * MOE_STEPS
N_QUARTERS = 4 * N_BLOCKS
N_HALVES = 2 * N_BLOCKS
WOUT_ORDER = ((0, 0), (0, 1), (1, 0), (1, 1), (0, 2), (0, 3), (1, 2), (1, 3))
WOUT2_ORDER = ((0, 0), (0, 1), (0, 2), (1, 0), (1, 1), (1, 2), (0, 3), (1, 3))


def feature_block(w):
    return [w[:, f * P:(f + 1) * P].reshape(-1, P, P).transpose(1, 0, 2).reshape(P, -1) for f in range(w.shape[1] // P)]


def token_block(w):
    return [w[2 * q * P:(2 * q + 2) * P].reshape(2, P, -1).transpose(1, 0, 2).reshape(P, -1) for q in range(4)]


def row_block(w):
    return [w[q * P:(q + 1) * P] for q in range(w.shape[0] // P)]


def weight_stream(a):
    w1, w2 = a["w_in"][0], a["w_in_2"][0]
    moba, ret, qs = HEADS * HD, RET_HEADS * P, []
    for i in range(2):
        qs += feature_block(w1[:, i * moba:(i + 1) * moba])
    qs += token_block(w1[:, 2 * moba:3 * moba])
    base = 3 * moba
    for i in range(2):
        qs += feature_block(w1[:, base + i * ret:base + (i + 1) * ret])
    for i in range(2, 4):
        qs += token_block(w1[:, base + i * ret:base + (i + 1) * ret])
    halves = [token_block(a["w_out"][0][:, i * 512:(i + 1) * 512]) for i in range(2)]
    qs += [halves[c][f] for c, f in WOUT_ORDER]

    up, gate, down = feature_block(a["w_up"][0]), feature_block(a["w_gate"][0]), row_block(a["w_down"][0])
    for i in range(FFN_STEPS):
        for f in (4 * i, 4 * i + 2):
            qs += up[f:f + 2] + gate[f:f + 2]
        qs += down[4 * i:4 * i + 4]
    f = 4 * FFN_STEPS
    ple = row_block(a["w_ple"][0])
    qs += up[f:] + gate[f:] + ple[:1] + down[f:] + ple[1:]
    for i in range(2):
        qs += token_block(a["w_ple_gate"][0][:, i * 512:(i + 1) * 512])

    col = {}
    at = 0
    for name, n in (("a_q", 512), ("a_k", 512), ("a_v", 512), ("a_z", 512), ("small", 16), ("b_q", 512), ("b_k", 128),
                    ("b_v", 128), ("i_q", 512), ("i_k", 64), ("i_w", 8), ("gate_a", D), ("gate_b", D)):
        col[name] = w2[:, at:at + n]
        at += n
    qs += feature_block(col["i_q"])
    kv = [col["b_k"][:, :HD], col["b_k"][:, :HD], col["b_k"][:, HD:], col["b_k"][:, HD:], col["i_k"], col["i_k"]]
    qs += feature_block(np.concatenate(kv + [col["b_v"]], axis=1)) + feature_block(col["b_q"])
    for name in ("a_q", "a_k", "a_v"):
        qs += feature_block(col[name])
    qs += token_block(col["a_z"]) + feature_block(col["gate_a"]) + feature_block(col["gate_b"])
    for name in ("w_proj_b_2", "w_proj_a_2"):
        tiles = feature_block(a[name][0])
        qs += [np.concatenate(tiles[i:i + 2], axis=1) for i in range(0, 8, 2)]
    halves = [token_block(a["w_out_2"][0][:, i * 512:(i + 1) * 512]) for i in range(2)]
    qs += [halves[c][f] for c, f in WOUT2_ORDER]
    for e in range(0, N_EXPERTS, 2):
        for x in (e, e + 1):
            qs += feature_block(a["w_exp_gate_2"][0, x]) + feature_block(a["w_exp_up_2"][0, x])
        qs += row_block(a["w_exp_down_2"][0, e]) + row_block(a["w_exp_down_2"][0, e + 1])
    assert len(qs) == N_QUARTERS
    out = np.empty((N_HALVES, P, 2 * QUARTER), np.float32)
    for q, w in enumerate(qs):
        out[q // 2, :, (q % 2) * QUARTER:(q % 2 + 1) * QUARTER] = w
    small = np.concatenate([col["small"], col["i_w"]], axis=1)
    router = np.concatenate([a["w_router_group_2"][0], a["w_router_expert_2"][0]], axis=1)
    smalls = [w.reshape(KD, P, -1).transpose(1, 0, 2).reshape(P, -1) for w in (small, router)]
    return out, np.ascontiguousarray(np.concatenate(smalls, axis=1))


DELTA_SCALAR = (2, 5, 8, 11, 13, 13, 16, 18, 18, 19)
DELTA_VECTOR = (7, 8, 11, 14, 18, 21, 22, 24, 25, 26)


def delta_slots():
    out = []
    for t in range(NT):
        out.append(("begin", t))
        out += [("stage", t, n) for n in range(10)]
        for c in (2 * t, 2 * t + 1):
            out += ([("old", c)] if c else []) + [("new", c)]
    return out


ATTENTION = 1536 + 4096 + 2 * KD * S
HEAD_TICK = 19
DELTA_SLOTS = delta_slots()
DELTA_START = 2 * (HEAD_TICK + 10)

def columns(*sizes):
    at, out = 0, {}
    for name, n in sizes:
        out[name] = slice(at, at + n)
        at += n
    return out, at


VEC, VEC_N = columns(("attn_norm", 8), ("ffn_norm", 8), ("ple_norm", 8), ("norm1", 8), ("norm2", 8), ("ret_norm", 4),
                     ("a_norm", 1), ("conv_b", FFN_TILES), ("b_gate", 2 * KD), ("conv_w", 3 * FFN_TILES), ("conv_w2", 4 * 12),
                     ("inv_freq", 1))
ROW, ROW_N = columns(("router_b", 20), ("a_log", 8), ("dt_bias", 8))
CON, CON_N = columns(("ident", P), ("rotate", P), ("head_sum", P), ("tri", P), ("upper", P), ("tri_c", CHUNK),
                     ("upper_c", CHUNK), ("near_c", CHUNK), ("far_c", CHUNK), ("ident_c", CHUNK), ("key_limit", P), ("chunk_ones", P), ("prior", N_EXPERTS), ("dist", S), ("decay", RET_HEADS * S))
CON_KEPT = CON["dist"].start


def vector_columns(a):
    def cols(v):
        return np.asarray(v).reshape(-1, P).T

    out = np.zeros((P, VEC_N), np.float32)
    for name, src in (("attn_norm", a["attn_norm"][0]), ("ffn_norm", a["ffn_norm"][0]), ("ple_norm", a["ple_norm"][0]),
                      ("norm1", a["norm1_g_2"][0]), ("norm2", a["norm2_g_2"][0]), ("ret_norm", a["ret_norm"][0]),
                      ("conv_b", a["conv_b"][0]), ("b_gate", a["b_gate_2"][0])):
        out[:, VEC[name]] = cols(src)
    out[:, VEC["a_norm"]] = np.concatenate([a["a_norm_g_2"][0]] * 2)[:, None]
    w = a["conv_w"][0]
    out[:, VEC["conv_w"]] = w.reshape(3, FFN_TILES, P).transpose(2, 1, 0).reshape(P, -1)
    w = a["conv_w_2"][0]
    out[:, VEC["conv_w2"]] = w.reshape(4, 12, P).transpose(2, 1, 0).reshape(P, -1)
    half = HD // 2
    inv = (np.float32(10000.0) ** (-np.arange(half, dtype=np.float32) / np.float32(half))).astype(np.float32)
    out[:, VEC["inv_freq"]] = np.tile(inv, 4)[:, None]
    return out


def shape_constants():
    i = np.arange(P)
    out = np.zeros((P, CON_N), np.float32)
    out[:, CON["ident"]] = np.eye(P)
    dist = P + i[:, None] - np.arange(S)[None, :]
    out[:, CON["dist"]] = np.where(dist >= 0, dist, BIG)
    log_g = np.log(1.0 - 2.0 ** (-5.0 - np.arange(RET_HEADS)))
    lag = np.arange(S)[None, :] - i[:, None]
    decay = np.where(lag[None] >= 0, np.exp(log_g[:, None, None] * np.maximum(lag, 0)[None]), 0.0) * P ** -0.5
    out[:, CON["decay"]] = decay.transpose(1, 0, 2).reshape(P, -1)
    rot = np.zeros((P, P))
    for f in range(P):
        if f % HD < HD // 2:
            rot[f + HD // 2, f] = -1.0
        else:
            rot[f - HD // 2, f] = 1.0
    out[:, CON["rotate"]] = rot
    out[:, CON["head_sum"]] = (i[:, None] // HD == i[None, :] // HD)
    same = i[:, None] // CHUNK == i[None, :] // CHUNK
    out[:, CON["tri"]] = same & (i[:, None] <= i[None, :])
    out[:, CON["upper"]] = same & (i[:, None] > i[None, :])
    row, column = i[:, None] % CHUNK, np.arange(CHUNK)[None, :]
    near = row // 16 == column // 16
    out[:, CON["tri_c"]] = row <= column
    out[:, CON["upper_c"]] = row > column
    out[:, CON["near_c"]] = near & (row > column)
    out[:, CON["far_c"]] = ~near & (row > column)
    out[:, CON["ident_c"]] = row == column
    out[:, CON["key_limit"]] = np.where((i[:, None] < CHUNK) & (i[None, :] >= CHUNK), -1e38, 0.0)
    out[:, CON["prior"]] = N_EXPERTS - np.arange(N_EXPERTS)
    out[:, CON["chunk_ones"]] = i[:, None] // CHUNK == i[None, :] // CHUNK
    return out


def program(nc, weights, smalls, x_in, p_in, vec_in, rows, con_in, sel_in, pos_in, out):
    ctx = ExitStack()
    with ctx:
        made = {}

        def sem(name):
            if name not in made:
                made[name] = ctx.enter_context(nc.semaphore(name))
            return made[name]

        def sb(name, cols, dt=F32):
            return ctx.enter_context(nc.sbuf_tensor(name, [P, cols], dt))

        raw = sb("raw", RING * QUARTER)
        w_hi = sb("w_hi", RING * QUARTER, F32R)
        w_lo = sb("w_lo", RING * QUARTER, F32R)
        h_hi = sb("h_hi", KD * S, F32R)
        h_lo = sb("h_lo", KD * S, F32R)
        g_hi = sb("g_hi", KD * S, F32R)
        g_lo = sb("g_lo", KD * S, F32R)
        p_hi = sb("p_hi", PLE_CHUNKS * S, F32R)
        p_lo = sb("p_lo", PLE_CHUNKS * S, F32R)
        sm_hi = sb("sm_hi", KD * 44, F32R)
        sm_lo = sb("sm_lo", KD * 44, F32R)
        h_hi, h_lo, g_hi, g_lo = (x[:, :].rearrange("p (k s) -> p k s", s=S) for x in (h_hi, h_lo, g_hi, g_lo))
        p_hi, p_lo = (x[:, :].rearrange("p (k s) -> p k s", s=S) for x in (p_hi, p_lo))

        x_sb = sb("x_sb", NT * D)
        x3 = x_sb[:, :].rearrange("p (t n) -> p t n", t=NT)
        tok = sb("tok", NT * D)
        tok3 = tok[:, :].rearrange("p (t n) -> p t n", t=NT)
        vec = sb("vec", VEC_N)
        row = sb("row", ROW_N)
        con = sb("con", CON_KEPT)
        stat = sb("stat", 160)
        work = sb("work", ARENA)

        def carve(at, *sizes):
            got = []
            for n in sizes:
                got.append(work[:, at:at + n])
                at += n
            assert at <= ARENA, at
            return got

        roots = stat[:, 64:96].rearrange("p (t n) -> p t n", t=NT)
        bank = [ctx.enter_context(nc.psum_tensor(f"bank{i}", [P, 512], F32)) for i in range(8)]
        ident = con[:, CON["ident"]]

        def v(name, i=0, n=1):
            return vec[:, VEC[name].start + i:VEC[name].start + i + n]

        (moba_p, moba_pt) = carve(0, 768, 768)
        (mq, mk, mv, rq, rk, rv, rg, rg_tanh, bias, ret_s, con1, p_raw, small_raw) = carve(
            1536, 1024, 1024, 1024, 1024, 1024, 1024, 1024, 1024, HEADS * S, 768, CON_N - CON_KEPT, PLE_CHUNKS * S, KD * 44)
        dist, decay = con1[:, 0:S], con1[:, S:]
        mq, mk, rq, rk = (a.rearrange("p (f s) -> p f s", s=S) for a in (mq, mk, rq, rk))
        mv, rv, rg, rg_tanh = (a.rearrange("p (t n) -> p t n", t=NT) for a in (mv, rv, rg, rg_tanh))
        bias = bias.rearrange("p (h s) -> p h s", s=S)
        (conv, act, ple, ple_tanh, norm_row) = carve(1536, 2 * 512, 2 * 512, NT * D, NT * 512, D)
        conv = conv.rearrange("p (b f s) -> p b f s", b=2, s=S)
        act = act.rearrange("p (b n) -> p b n", b=2)
        ple3 = ple.rearrange("p (t n) -> p t n", t=NT)
        ple_tanh = ple_tanh.rearrange("p (t n) -> p t n", t=NT)

        cos, sin = carve(ARENA - 512, S, S)
        (angle, turns) = carve(ARENA - 1024, S, S)
        (aq, ak, av, az, gates) = carve(1536, 1024, 1024, 1024, 1024, 2 * KD * S)
        aq, ak, av, gates = (a.rearrange("p (f s) -> p f s", s=S) for a in (aq, ak, av, gates))
        az = az.rearrange("p (t n) -> p t n", t=NT)
        (bq, iq, bk, ik, bv, rope_tmp, relu, index, masks) = carve(
            ATTENTION, 1024, 1024, 512, S, S, 1024, 1024, NT * S, NT * S)
        (ik_bv,) = carve(ATTENTION + 2560, 512)
        bq, iq, bk, ik = (a.rearrange("p (f s) -> p f s", s=S) for a in (bq, iq, bk, ik))
        bv = bv.rearrange("p (t n) -> p t n", t=NT)
        rope_tmp, relu = (a.rearrange("p (b n) -> p b n", b=2) for a in (rope_tmp, relu))
        index, masks = (a.rearrange("p (t n) -> p t n", t=NT) for a in (index, masks))
        silu_tanh = carve(ATTENTION + 6144, 1024)[0].rearrange("p (b n) -> p b n", b=2)
        squares = carve(ATTENTION + 3072, 2048)[0].rearrange("p (b n) -> p b n", b=4)
        roots_wide = carve(ATTENTION + 3072, 2048)[0].rearrange("p (t n) -> p t n", t=NT)
        kinds = (("near_d", 512), ("near_td", 512), ("sq_d", 512), ("inv_td", 512), ("far_d", 512), ("near_c", S),
                 ("near_tc", S), ("sq_c", S), ("sq_tc", S), ("inv_tc", S), ("far_c", S))
        delta = []
        for g in range(2):
            parts = carve(ATTENTION + 4096 * g, *[n for _, n in kinds])
            delta.append({name: x.rearrange("p (m c) -> p m c", m=4) for (name, _), x in zip(kinds, parts)})
            (y,) = carve(ATTENTION + 4096 * g + 3072, 512)
            delta[g]["y"] = y.rearrange("p (m c) -> p m c", m=4)
        diagonal = [carve(ATTENTION + 4096 * g, 5 * 512)[0].rearrange("p (n c) -> p n c", c=P) for g in range(2)]
        v_new, o_tmp = (carve(ATTENTION + 4096 * g + 3072, 512)[0].rearrange("p (g n) -> p g n", g=2) for g in range(2))
        g_upper, g_tri = (carve(ATTENTION + 4096 * g + 3072, 512)[0].rearrange("p (h c) -> p h c", c=CHUNK)
                          for g in range(2))
        state, qk_t = carve(ATTENTION + 8192, S, 512)
        qk_t = qk_t.rearrange("p (g m c) -> p g m c", g=2, c=CHUNK)
        r_sb, k_dec = carve(0, 1024, 512)
        r_sb = r_sb.rearrange("p (h c) -> p h c", c=P)
        k_dec = k_dec.rearrange("p (h c) -> p h c", c=HD)
        u_sb, w_t = carve(0, 512, 512)
        u_sb = u_sb.rearrange("p (g n) -> p g n", g=2)
        w_t = w_t.rearrange("p (m c) -> p m c", c=P)
        (o_squares,) = carve(ATTENTION, 1024)
        (combs, e_act) = carve(1536, N_EXPERTS * S, 1024)
        (selectors,) = carve(ATTENTION + 2048, N_EXPERTS * P)
        e_act = e_act.rearrange("p (b n) -> p b n", b=2)
        (norm_row2,) = carve(ARENA - D, D)
        (comb, comb_t, route) = carve(1536 + N_EXPERTS * S + 1024, NT * N_EXPERTS, S, 354)
        comb, comb_t = comb.rearrange("p (t e) -> p t e", t=NT), comb_t[0:N_EXPERTS, :]
        small_tok = sb("small_tok", NT * 24)[:, :].rearrange("p (t n) -> p t n", t=NT)
        (beta, beta_half, decay_g, index_w, soft_a, soft_b) = (
            sb(n, NT * HEADS)[:, :].rearrange("p (t h) -> p t h", t=NT)
            for n in ("beta", "beta_half", "decay_g", "index_w", "soft_a", "soft_b"))
        rate = sb("rate", HEADS)
        gate_bias = sb("gate_bias", 2 * KD)
        exp_g = sb("exp_g", 24)
        beta_g = sb("beta_g", HEADS)
        best = sb("best", NT * 8)
        root_bias = sb("root_bias", 2)

        def routes(at, n):
            return route[:, at:at + n].rearrange("p (t n) -> p t n", t=NT)

        logits, keys, first, second, masked = (routes(64 * i, NT * n) for i, n in enumerate((20, 16, 16, 16, 16)))
        group_one, group_exp, second_exp = routes(320, 8), routes(328, 8), route[:, 336:338]
        group_max, group_sum, best_key, top, top2, w_first, w_second = (route[:, 340 + 2 * i:342 + 2 * i] for i in range(7))

        def halves_of(x, chunk):
            rows = slice(CHUNK * chunk, CHUNK * (chunk + 1))
            return x[rows, :, CHUNK * chunk:CHUNK * (chunk + 1)] if x.shape[2] == P else x[rows, :, :]

        def bank_part(i, at, c):
            return bank[i][:, at:at + 4 * c].rearrange("p (m c) -> p m c", c=c)

        def delta_slot(half, run):
            n = half - DELTA_START
            if 0 <= n < len(DELTA_SLOTS):
                run(*DELTA_SLOTS[n])

        block = ctx.enter_context(nc.Block())

        def ring(q):
            return slice(q % RING * QUARTER, (q % RING + 1) * QUARTER)

        def pair(u):
            return bank[2 * (u % 2)], bank[2 * (u % 2) + 1]

        @block.sync
        def _(sp):
            for t in range(NT):
                sp.dma_start(x3[:, t, :], x_in[t * P:(t + 1) * P, :]).then_inc(sem("x_loaded"), 16)

            def load_half(half, slot):
                src = weights[bass.ds(half, 1), :, :].rearrange("a p n -> (a p) n")
                sp.dma_start(raw[:, 2 * slot * QUARTER:(2 * slot + 2) * QUARTER], src)\
                    .then_inc(sem(f"half_loaded{slot}"), 16)

            for half in range(3):
                load_half(half, half)
            with sp.Fori(0, N_HALVES // 3 - 1) as i:
                for slot in range(3):
                    sp.wait_ge(sem("lo_done"), i * 6 + 2 * slot + 2)
                    load_half(i * 3 + (3 + slot), slot)
            for half in range(N_HALVES - N_HALVES % 3, N_HALVES):
                sp.wait_ge(sem("lo_done"), 2 * half - 4)
                load_half(half, half % 3)
            sp.wait_ge(sem("final_ready"), NT)
            sp.dma_start(out.rearrange("(t p) n -> p t n", p=P), tok3).then_inc(sem("stored"), 16)
            sp.wait_ge(sem("stored"), 16)

        @block.gpsimd
        def _(pool):
            def lo(n, r):
                pool.wait_ge(sem("hi_done"), n + 1)
                nc.gpsimd.tensor_tensor(w_lo[:, ring(r)], raw[:, ring(r)], w_hi[:, ring(r)].bitcast(F32),
                                        ALU.subtract).then_inc(sem("lo_done"), 1)

            with pool.Fori(0, N_QUARTERS // RING) as i:
                for r in range(RING):
                    lo(i * RING + r, r)
            for n in range(N_QUARTERS - N_QUARTERS % RING, N_QUARTERS):
                lo(n, n)

        @block.scalar
        def _(act_e):
            for dst, src in ((ident, con_in[:, CON["ident"]]), (vec[:, :], vec_in)):
                act_e.dma_start(dst, src).then_inc(sem("first_constants"), 16)

            def load_constants():
                for dst, src in ((con[:, P:CON_KEPT], con_in[:, P:CON_KEPT]), (con1, con_in[:, CON_KEPT:]),
                                 (small_raw[:, :], smalls), (p_raw, p_in)):
                    act_e.dma_start(dst, src).then_inc(sem("constants_loaded"), 16)
                act_e.dma_start(turns.bitcast(I32), pos_in.partition_broadcast(P)).then_inc(sem("positions_loaded"), 16)
                for name in ("router_b", "a_log", "dt_bias"):
                    act_e.dma_start(row[:, ROW[name]], rows[name].partition_broadcast(P))\
                        .then_inc(sem("constants_loaded"), 16)


            def hi(q, base=0):
                n = base + q
                if isinstance(n, int) and n >= N_QUARTERS:
                    return
                act_e.wait_ge(sem(f"half_loaded{q % RING // 2}"), (base // RING + q // RING + 1) * 16)
                if not isinstance(n, int) or n >= RING:
                    act_e.wait_ge(sem("quarter_done"), n - (RING - 1))
                nc.scalar.activation(w_hi[:, ring(q)], raw[:, ring(q)], ACT.Copy).then_inc(sem("hi_done"), 1)

            def second_squares():
                nc.scalar.activation(tok3[:, 1, :], x3[:, 1, :], ACT.Square, scale=D ** -0.5, accum_out=stat[:, 1:2])\
                    .then_inc(sem("second_squares"), 1)

            def norm_hi(n, gain):
                for k in range(KD):
                    act_e.wait_ge(sem("norm_turned"), 4 * n + k // 2 + 1)
                    nc.scalar.activation(h_hi[:, k, :], bank[4 + k // 2][:, (k % 2) * S:(k % 2 + 1) * S], ACT.Copy,
                                         scale=v(gain, k)).then_inc(sem("h_hi_done"), 1)

            def exp(n):
                p = moba_p[:, n % 2 * 384:(n % 2 + 1) * 384]
                for t, part in ((0, p[:, 0:P]), (1, p[:, P:384])):
                    act_e.wait_ge(sem("negated_ready"), 2 * n + t + 1)
                    i = 2 * (n % HEADS) + t
                    nc.scalar.activation(part, part, ACT.Exp, bias=stat[:, 32 + i:33 + i], scale=-1.0,
                                         accum_out=stat[:, 48 + i:49 + i]).then_inc(sem("p_ready"), 1)

            def p_turned_copy(n):
                act_e.wait_ge(sem("p_turned"), n + 1)
                if n >= 2:
                    act_e.wait_ge(sem("head_out"), n - 1)
                nc.scalar.copy(moba_pt[:, n % 2 * 384:(n % 2 + 1) * 384], bank[6 + n % 2][:, 0:384])\
                    .then_inc(sem("pt_ready"), 1)

            act_e.wait_ge(sem("x_loaded"), 16 * NT)
            second_squares()
            for q in range(LEAD):
                hi(q)
            act_e.wait_ge(sem("first_constants"), 32)
            norm_hi(0, "attn_norm")
            load_constants()
            for q in range(4 * B_WOUT):
                tick = q - 4 * B_RQ
                if q == 8:
                    act_e.wait_ge(sem("angles_ready"), 2)
                    nc.scalar.activation(cos, angle, ACT.Sin)
                    nc.scalar.activation(sin, turns, ACT.Sin).then_inc(sem("rope_tables"), 1)
                if 1 <= tick <= HEADS:
                    p_turned_copy(tick - 1)
                hi(q + LEAD)
                if 0 <= tick < HEADS:
                    exp(tick)
            def mix_hi(k, n, gain=None):
                act_e.wait_ge(sem("mix_turned"), n // 2 + 1)
                src = bank[4 + k // 2][:, (k % 2) * S:(k % 2 + 1) * S]
                nc.scalar.activation(g_hi[:, k, :], src, ACT.Copy, scale=1.0 if gain is None else gain)\
                    .then_inc(sem("mix_hi_done"), 1)

            for k in range(4):
                mix_hi(k, k)
            for t in range(NT):
                act_e.wait_ge(sem("quarter_done"), 4 * B_RG + 4)
                nc.scalar.activation(rg_tanh[:, t, :], pair(6)[t][:, :], ACT.Tanh, scale=0.5)\
                    .then_inc(sem("rg_tanh_ready"), 1)
            for q in range(4 * B_WOUT, 4 * B_WOUT + 3):
                hi(q + LEAD)
            for k in range(4, 8):
                mix_hi(k, k, v("ret_norm", k - 4))
            for q in range(4 * B_WOUT + 3, 4 * B_FFN):
                hi(q + LEAD)
            act_e.wait_ge(sem("pair_free1"), 8)
            act_e.wait_ge(sem("pair_free0"), 10)
            second_squares()
            norm_hi(1, "ffn_norm")
            act_e.dma_start(norm_row, rows["final_norm"].partition_broadcast(P)).then_inc(sem("norm_row_loaded"), 16)

            def conv_first(b, i, n_up, f):
                for j in range(2):
                    act_e.wait_ge(sem("quarter_done"), b + 2)
                    nc.scalar.activation(conv[:, i, j, :], pair_u[i][0][:, j * S:(j + 1) * S], ACT.Identity,
                                         bias=fvec("conv_b", f + j), scale=fvec("conv_w", (f + j) * 3 + 2))\
                        .then_inc(sem("conv_first"), 1)

            def fvec(name, i):
                return vec[:, bass.ds(i + VEC[name].start, 1)]

            pair_u = [pair(1), pair(0)]

            def gelu(i, n_up):
                act_e.wait_ge(sem(f"pair_free{1 - i}"), n_up - i + 9 + 2 * i)
                nc.scalar.activation(act[:, i, :], conv[:, i, :, :], ACT.Gelu_apprx_tanh).then_inc(sem("gelu_done"), 1)

            def act_hi(i, n_up):
                act_e.wait_ge(sem(f"pair_free{1 - i}"), n_up - i + 10 + 2 * i)
                nc.scalar.copy(g_hi[:, 2 * i:2 * i + 2, :], act[:, i, :]).then_inc(sem("act_hi_done"), 1)

            def ffn_up(i, q0, base, n_up, f):
                for q in range(4):
                    hi(q0 + q + LEAD, base)
                    if q == 1:
                        conv_first(base + q0, i, n_up, f)
                gelu(i, n_up)
                act_hi(i, n_up)

            def ffn_step(base, n, f):
                ffn_up(0, 0, base, n, f)
                ffn_up(1, 4, base, n + 1, f + 2)
                for q in range(8, 12):
                    hi(q + LEAD, base)

            assert 4 * B_FFN % RING == 0 and 4 * B_FFN_LAST % RING == 0
            ffn_step(4 * B_FFN, 0, 0)
            with act_e.Fori(1, FFN_STEPS) as i:
                ffn_step(i * 12 + 4 * B_FFN, i * 2, i * 4)
            ffn_up(0, 0, 4 * B_FFN_LAST, 2 * FFN_STEPS, 4 * FFN_STEPS)
            for q in range(4 * B_PLE_DOWN, 4 * B_PLE_GATE):
                hi(q + LEAD)
            act_e.wait_ge(sem("x_summed"), 4)
            second_squares()
            norm_hi(2, "ple_norm")
            for q in range(4 * B_PLE_GATE, 4 * B_IQ):
                hi(q + LEAD)
            for n in range(2):
                for t in range(NT):
                    act_e.wait_ge(sem("quarter_done"), 4 * (B_PLE_GATE + n) + 4)
                    if n == 1:
                        act_e.wait_ge(sem("ple_added"), t + 1)
                    nc.scalar.activation(ple_tanh[:, t, :], pair(22 + n)[t][:, :], ACT.Tanh, scale=0.5)\
                        .then_inc(sem(f"pair_free{n}"), 1)

            act_e.wait_ge(sem("ple_added"), 2 * NT)
            second_squares()

            act_e.wait_ge(sem("first_out"), NT)
            second_squares()
            norm_hi(3, "norm1")

            def store(b, u, dsts):
                for i, dst in enumerate(dsts):
                    act_e.wait_ge(sem("quarter_done"), 4 * b + 4)
                    nc.scalar.copy(dst, pair(u)[i][:, :]).then_inc(sem(f"pair_free{u % 2}"), 1)

            def conv2_first(n, dst):
                for f in range(4):
                    act_e.wait_ge(sem("quarter_done"), 4 * (B_AQ + n) + 4)
                    nc.scalar.activation(dst[:, f, :], pair(27 + n)[f // 2][:, f % 2 * S:(f % 2 + 1) * S], ACT.Copy,
                                         scale=v("conv_w2", (4 * n + f) * 4 + 3)).then_inc(sem("conv2_first"), 1)

            def silu2(n, src):
                for i in range(2):
                    u = 27 + n
                    act_e.wait_ge(sem(f"pair_free{u % 2}"), 2 * (u // 2) + i + 1)
                    if n:
                        act_e.wait_ge(sem("silu_done"), 2 * (n - 1) + i + 1)
                    nc.scalar.activation(silu_tanh[:, i, :], src[:, 2 * i:2 * i + 2, :], ACT.Tanh, scale=0.5)\
                        .then_inc(sem("silu_tanh_ready"), 1)

            def index_relu(x):
                for odd in range(2):
                    act_e.wait_ge(sem("index_scores"), 2 * x + odd + 1)
                    if x:
                        act_e.wait_ge(sem("index_added"), (0, 8, 12)[x])
                    nc.scalar.activation(relu[:, odd, :], bank[4 + odd][:, :], ACT.Relu).then_inc(sem("index_relu"), 1)

            def gate_tanh(i):
                for f in range(4):
                    act_e.wait_ge(sem("quarter_done"), 4 * (B_GATES + i) + 4)
                    k = 4 * i + f
                    ins = nc.scalar.activation(gates[:, k, :], pair(31 + i)[f // 2][:, f % 2 * S:(f % 2 + 1) * S], ACT.Tanh,
                                               scale=0.5, bias=gate_bias[:, k:k + 1])
                    if f % 2:
                        ins.then_inc(sem(f"pair_free{(31 + i) % 2}"), 1)

            act_e.wait_ge(sem("gate_bias_ready"), 1)

            def merged_hi(f):
                act_e.wait_ge(sem("merged"), f + 1)
                nc.scalar.activation(h_hi[:, 2 * f:2 * f + 2, :], gates[:, 2 * f:2 * f + 2, :], ACT.Copy, scale=0.5)\
                    .then_inc(sem("merged_hi_done"), 1)

            def delta_stage(t, stage, g):
                d, n, b = delta[g], sem(f"delta_scalar{g}"), 4 + 2 * g
                first, both = bank_part(b, 0, CHUNK), bank_part(b, 0, P)
                if stage in (5, 8):
                    return
                act_e.wait_ge(sem(f"delta_ready{g}"), 10 * t + stage + 1)

                def copy(dst, src, how=ACT.Copy):
                    nc.scalar.activation(dst, src, how).then_inc(n, 1)

                def to_diagonal(name):
                    for c in range(2):
                        copy(halves_of(d[name], c), halves_of(first, c))

                if stage == 0:
                    copy(d["near_tc"], first, ACT.Exp)
                    copy(d["inv_tc"], bank_part(b, S, CHUNK), ACT.Exp)
                elif stage == 1:
                    for c in range(2):
                        copy(halves_of(d["near_tc"], c), halves_of(both, c))
                    copy(d["near_td"], both)
                elif stage == 2:
                    copy(d["sq_c"], first)
                    to_diagonal("sq_d")
                elif stage == 3:
                    copy(d["near_c"], first)
                    to_diagonal("near_d")
                elif stage in (4, 7):
                    to_diagonal("sq_d")
                elif stage == 6:
                    copy(d["near_tc"], bank_part(b, S, CHUNK))
                    to_diagonal("near_d")
                elif stage == 9:
                    own = slice(HD * g, HD * g + HD)
                    copy(w_t[own, :, :], both[own, :, :])

            def delta_step(kind, n, stage=None):
                if kind == "begin":
                    act_e.wait_ge(sem("prelude_ready"), n + 1)
                    nc.scalar.activation(exp_g[:, :], bank[6][:, 0:24], ACT.Exp).then_inc(sem("exp_g_ready"), 1)
                elif kind == "stage":
                    for g in range(2):
                        delta_stage(n, stage, g)

            def root():
                act_e.wait_ge(sem("square_sums"), 1)
                act_e.wait_ge(sem("root_bias_ready"), 1)
                sums = bank[4][:, 0:32].rearrange("p (t n) -> p t n", t=NT)
                for i in range(2):
                    of = slice(8 * i, 8 * i + 8)
                    nc.scalar.activation(roots[:, :, of], sums[:, :, of], ACT.Sqrt, scale=(float(HD), 1.0)[i],
                                         bias=root_bias[:, i:i + 1]).then_inc(sem("rooted"), 1)

            for q in range(4 * B_IQ, 4 * B_WOUT2):
                tick = q - 4 * B_IQ
                if tick == 2:
                    act_e.wait_ge(sem("constants_loaded"), 16 * N_CONSTANT_LOADS)
                    act_e.wait_ge(sem("soft_in_ready"), 1)
                    nc.scalar.activation(beta[:, :, :], small_tok[:, :, 0:8], ACT.Tanh, scale=0.5)
                    nc.scalar.activation(rate[:, :], row[:, ROW["a_log"]], ACT.Exp)
                    nc.scalar.activation(soft_b[:, :, :], soft_b[:, :, :], ACT.Exp).then_inc(sem("soft_exp"), 1)
                    act_e.wait_ge(sem("soft_exp"), 1)
                    nc.scalar.activation(soft_b[:, :, :], soft_b[:, :, :], ACT.Ln, bias=1.0).then_inc(sem("soft_ready"), 1)
                if tick == 4:
                    store(B_IQ, 24, (iq[:, 0:2, :], iq[:, 2:4, :]))
                if tick == 8:
                    store(B_KV, 25, (bk[:, :, :], ik_bv))
                if tick == 12:
                    store(B_BQ, 26, (bq[:, 0:2, :], bq[:, 2:4, :]))
                if tick in (16, 20, 24):
                    n = (tick - 16) // 4
                    conv2_first(n, (aq, ak, av)[n])
                if tick == 4 * (B_PROJ + 1 - B_IQ):
                    for k in range(4):
                        mix_hi(k, 12 + k, v("a_norm"))
                delta_slot(2 * tick, delta_step)
                hi(q + LEAD)
                delta_slot(2 * tick + 1, delta_step)
                if tick in (12, 13, 14):
                    index_relu(tick - 12)
                if tick in (18, 22, 26):
                    n = (18, 22, 26).index(tick)
                    silu2(n, (aq, ak, av)[n])
                if tick == 25:
                    for i in range(4):
                        act_e.wait_ge(sem("silu_done"), 4)
                        nc.scalar.square(squares[:, i, :], (aq, ak)[i // 2][:, 2 * (i % 2):2 * (i % 2) + 2, :])\
                            .then_inc(sem("squared"), 1)
                if tick == 28:
                    for t in range(NT):
                        act_e.wait_ge(sem("quarter_done"), 4 * B_AZ + 4)
                        nc.scalar.activation(tok3[:, t, 0:512], pair(30)[t][:, :], ACT.Tanh, scale=0.5)\
                            .then_inc(sem("az_tanh_ready"), 1)
                if 1 <= tick - HEAD_TICK <= HEADS:
                    p_turned_copy(HEADS + tick - HEAD_TICK - 1)
                if 0 <= tick - HEAD_TICK < HEADS:
                    exp(HEADS + tick - HEAD_TICK)
                if tick == HEAD_TICK + HEADS:
                    root()
                if tick == HEAD_TICK + HEADS + 1:
                    for k in range(4, 8):
                        mix_hi(k, 4 + k)
                if tick >= 32 and tick % 4 == 0 and tick < 48:
                    gate_tanh((tick - 32) // 4)
                if q >= 4 * (B_PROJ + 1) + 1:
                    merged_hi(q - 4 * (B_PROJ + 1) - 1)
            merged_hi(3)
            act_e.dma_start(selectors[0:N_EXPERTS, :], sel_in).then_inc(sem("selectors_loaded"), 16)
            act_e.dma_start(norm_row2, rows["final_norm_2"].partition_broadcast(P)).then_inc(sem("norm_row2_loaded"), 16)
            for q in range(4 * B_WOUT2, 4 * B_MOE):
                hi(q + LEAD)
            act_e.wait_ge(sem("pair_free1"), 40)
            act_e.wait_ge(sem("pair_free0"), 42)
            second_squares()
            norm_hi(4, "norm2")

            def expert_up(base, q0, i, n):
                for q in range(4):
                    hi(q0 + q + LEAD, base)
                    if q == 1:
                        act_e.wait_ge(sem("quarter_done"), base + q0 + 2)
                        nc.scalar.activation(e_act[:, i, :], pair_u[i][0][:, :], ACT.Silu)\
                            .then_inc(sem(f"pair_free{1 - i}"), 1)
                act_e.wait_ge(sem("expert_act_ready"), n + 1)
                nc.scalar.copy(g_hi[:, 2 * i:2 * i + 2, :], e_act[:, i, :]).then_inc(sem("expert_hi_done"), 1)

            def expert_step(base, n, last=False):
                expert_up(base, off, 0, n)
                expert_up(base, off + 4, 1, n + 1)
                for q in range(8, 12):
                    if not last or q + LEAD < 12:
                        hi(off + q + LEAD, base)

            off = 4 * B_MOE % RING
            base = 4 * B_MOE - off
            for q in range(4):
                hi(base + off + q + LEAD)
            act_e.wait_ge(sem("group_in_ready"), 1)
            nc.scalar.activation(group_exp, group_exp, ACT.Exp).then_inc(sem("group_exp"), 1)
            act_e.wait_ge(sem("second_in_ready"), 1)
            nc.scalar.activation(second_exp, second_exp, ACT.Exp).then_inc(sem("second_exp"), 1)
            for q in range(4, 8):
                hi(base + off + q + LEAD)
            for i in range(2):
                act_e.wait_ge(sem("quarter_done"), base + off + 4 * i + 2)
                nc.scalar.activation(e_act[:, i, :], pair_u[i][0][:, :], ACT.Silu).then_inc(sem(f"pair_free{1 - i}"), 1)
            for i in range(2):
                act_e.wait_ge(sem("expert_act_ready"), i + 1)
                nc.scalar.copy(g_hi[:, 2 * i:2 * i + 2, :], e_act[:, i, :]).then_inc(sem("expert_hi_done"), 1)
            for q in range(8, 12):
                hi(base + off + q + LEAD)
            with act_e.Fori(1, MOE_STEPS - 1) as i:
                expert_step(i * 12 + base, i * 2)
            expert_step(base + 12 * (MOE_STEPS - 1), 2 * (MOE_STEPS - 1), True)
            act_e.wait_ge(sem("x_summed"), 8)
            second_squares()

        @block.tensor
        def _(pe):
            mm = nc.tensor.matmul

            def three(dst, w, h, start, stop, weight_stationary):
                passes = ((0, 0), (0, 1), (1, 0)) if weight_stationary else ((0, 0), (1, 0), (0, 1))
                for n, (i, j) in enumerate(passes):
                    a, b = (w[i], h[j]) if weight_stationary else (h[j], w[i])
                    ins = mm(dst, a, b, start=start and n == 0, stop=stop and n == 2, skip_group_check=True)
                return ins

            def quarter(q):
                return w_hi[:, ring(q)], w_lo[:, ring(q)]

            def await_quarter(n):
                pe.wait_ge(sem("lo_done"), n + 1)

            def await_pair(u):
                if u >= 2:
                    pe.wait_ge(sem(f"pair_free{u % 2}"), 2 * (u // 2))

            def await_read(u):
                pe.wait_ge(sem(f"pair_free{u % 2}"), 2 * (u // 2) + 2)

            def feature_quarter(n, q, dst, h=(h_hi, h_lo), norm=None, middle=None):
                await_quarter(n)
                w = [x.rearrange("p (k c) -> p k c", c=P) for x in quarter(q)]
                for k in range(KD):
                    if middle and k == KD // 2:
                        middle()
                    if norm is not None:
                        pe.wait_ge(sem("h_lo_done"), KD * norm + k + 1)
                    ins = three(dst, [x[:, k, :] for x in w], [x[:, k, :] for x in h], k == 0, k == KD - 1, True)
                ins.then_inc(sem("quarter_done"), 1)

            def feature_project(b, u, beside=lambda f: None, norm=None, middle=lambda f: None):
                await_pair(u)
                for f in range(4):
                    beside(f)
                    q = 4 * b + f
                    feature_quarter(q, q, pair(u)[f // 2][:, f % 2 * S:(f % 2 + 1) * S], norm=None if f else norm,
                                    middle=lambda: middle(f))

            def token_quarter(q, u, f, h):
                await_quarter(q)
                w = [x.rearrange("p (k c) -> p k c", c=512) for x in quarter(q)]
                for t in range(NT):
                    for j in range(2):
                        k = 2 * f + j
                        ins = three(pair(u)[t][:, :], [x[:, j, :] for x in w],
                                    [x[:, k, t * P:(t + 1) * P] for x in h], k == 0, k == KD - 1, False)
                ins.then_inc(sem("quarter_done"), 1)

            def token_project(b, u, h=(h_hi, h_lo), beside=lambda f: None, norm=None):
                await_pair(u)
                for f in range(4):
                    beside(f)
                    if norm is not None:
                        pe.wait_ge(sem("h_lo_done"), KD * norm + 2 * f + 2)
                    token_quarter(4 * b + f, u, f, h)

            def row_quarter(n, q, banks, h, k, start, stop):
                await_quarter(n)
                w = quarter(q)
                for t in range(NT):
                    for c in range(2):
                        ins = three(banks[2 * t + c][:, :], [x[:, c * 512:(c + 1) * 512] for x in w],
                                    [x[:, k, t * P:(t + 1) * P] for x in h], start, stop, False)
                ins.then_inc(sem("quarter_done"), 1)

            def norm_turn(n):
                for k in range(KD):
                    for t in range(NT):
                        if k == 0:
                            pe.wait_ge(sem("x_normed"), NT * n + t + 1)
                        ins = nc.tensor.transpose(bank[4 + k // 2][:, k % 2 * S + t * P:k % 2 * S + (t + 1) * P],
                                                  tok3[:, t, k * P:(k + 1) * P], ident)
                    if k % 2:
                        ins.then_inc(sem("norm_turned"), 1)

            def scores(n, q3, k3, kf):
                f, at = n % HEADS // 2, HD * (n % 2)
                if n >= 2:
                    pe.wait_ge(sem("negated_ready"), 2 * (n - 1))
                for t in range(NT):
                    ins = mm(bank[4 + n % 2][:, t * P:t * P + (t + 1) * P], q3[at:at + HD, f, t * P:(t + 1) * P],
                             k3[at:at + HD, kf(f), 0:(t + 1) * P], start=True, stop=True)
                ins.then_inc(sem("scores_ready"), 1)

            def turn_p(n):
                p = moba_p[:, n % 2 * 384:(n % 2 + 1) * 384]
                pe.wait_ge(sem("p_ready"), 2 * n + 2)
                if n >= 2:
                    pe.wait_ge(sem("head_stored"), 2 * (n - 1))
                for i in range(3):
                    ins = nc.tensor.transpose(bank[6 + n % 2][:, i * P:(i + 1) * P], p[:, i * P:(i + 1) * P], ident)
                ins.then_inc(sem("p_turned"), 1)

            def head_out(n, v3, at):
                pt = moba_pt[:, n % 2 * 384:(n % 2 + 1) * 384]
                o = bank[6 + n % 2]
                pe.wait_ge(sem("pt_ready"), n + 1)
                mm(o[:, 384:448], pt[:, 0:P], v3[:, 0, at:at + HD], start=True, stop=True)
                mm(o[:, 448:512], pt[:, P:2 * P], v3[:, 0, at:at + HD], start=True, stop=False)
                mm(o[:, 448:512], pt[:, 2 * P:384], v3[:, 1, at:at + HD], start=False, stop=True)\
                    .then_inc(sem("head_out"), 1)

            def ret_scores(h):
                if h == 0:
                    pe.wait_ge(sem("negated_ready"), 2 * HEADS)
                elif h >= 2:
                    pe.wait_ge(sem("ret_s_ready"), 2 * (h - 1))
                s = bank[4 + h % 2]
                mm(s[:, 0:S], rk[:, h, 0:P], rq[:, h, :], start=True, stop=True)
                mm(s[:, S:384], rk[:, h, P:S], rq[:, h, P:S], start=True, stop=True).then_inc(sem("ret_scores"), 1)

            def ret_out(h):
                s = ret_s[:, h % 2 * 384:(h % 2 + 1) * 384]
                o = bank[6 + h // 2][:, h % 2 * S:(h % 2 + 1) * S]
                if h == 0:
                    pe.wait_ge(sem("head_stored"), 2 * HEADS)
                    await_read(5)
                pe.wait_ge(sem("ret_s_ready"), 2 * h + 2)
                e = slice(h * P, (h + 1) * P)
                mm(o[:, 0:P], s[:, 0:P], rv[:, 0, e], start=True, stop=True)
                mm(o[:, P:S], s[:, P:S], rv[:, 0, e], start=True, stop=False)
                mm(o[:, P:S], s[:, S:384], rv[:, 1, e], start=False, stop=True).then_inc(sem("ret_out"), 1)

            pe.wait_ge(sem("first_constants"), 32)
            norm_turn(0)
            feature_project(B_MQ, 0, norm=0)
            feature_project(B_MK, 1)
            token_project(B_MV, 2)

            def beside_first(tick):
                if tick == 0:
                    await_read(0)
                    await_read(1)
                if 1 <= tick <= HEADS:
                    turn_p(tick - 1)
                if tick < HEADS:
                    scores(tick, mq, mk, lambda f: f)
                if tick == 2:
                    await_read(2)
                if 2 <= tick < HEADS + 2:
                    head_out(tick - 2, mv, HD * (tick - 2))
                if tick == 10:
                    await_read(3)
                    await_read(4)
                    ret_scores(0)
                if tick == 11:
                    ret_scores(1)
                if tick == 13:
                    ret_out(0)
                    ret_scores(2)
                if tick == 14:
                    ret_out(1)
                    ret_scores(3)
                if tick == 15:
                    ret_out(2)
                    pe.wait_ge(sem("ret_s_ready"), 2 * RET_HEADS)
                    mix_turn(0)

            def mix_turn(k0):
                for k in range(k0, k0 + 4):
                    for t in range(NT):
                        ins = nc.tensor.transpose(bank[4 + k // 2][:, k % 2 * S + t * P:k % 2 * S + (t + 1) * P],
                                                  tok3[:, t, k * P:(k + 1) * P], ident)
                    if k % 2:
                        ins.then_inc(sem("mix_turned"), 1)

            feature_project(B_RQ, 3, lambda f: beside_first(f))
            feature_project(B_RK, 4, lambda f: beside_first(4 + f))
            token_project(B_RV, 5, beside=lambda f: beside_first(8 + f))
            token_project(B_RG, 6, beside=lambda f: beside_first(12 + f))
            ret_out(3)
            for n, (c, f) in enumerate(WOUT_ORDER):
                if f == 0:
                    await_pair(7 + c)
                if n == 3:
                    pe.wait_ge(sem("ret_gated"), NT)
                    mix_turn(4)
                pe.wait_ge(sem("mix_lo_done"), 2 * f + 2)
                token_quarter(4 * B_WOUT + n, 7 + c, f, (g_hi, g_lo))
            norm_turn(1)

            def up_block(base, q0, i, free, norm=None):
                pe.wait_ge(sem(f"pair_free{1 - i}"), free)
                for f in range(4):
                    feature_quarter(base + q0 + f, q0 + f, pair(1 - i)[f // 2][:, f % 2 * S:(f % 2 + 1) * S],
                                    norm=None if f else norm)

            def down_block(base, q0, n_up, start, stop, count=4):
                for k in range(count):
                    if k % 2 == 0:
                        pe.wait_ge(sem("act_lo_done"), n_up + k // 2 + 1)
                    row_quarter(base + q0 + k, q0 + k, bank[4:8], (g_hi, g_lo), k, start and k == 0,
                                stop and k == count - 1)

            def ffn_step(base, n, start):
                up_block(base, 0, 0, n + 8, 1 if start else None)
                up_block(base, 4, 1, n + 10)
                down_block(base, 8, n, start, False)

            ffn_step(4 * B_FFN, 0, True)
            with pe.Fori(1, FFN_STEPS) as i:
                ffn_step(i * 12 + 4 * B_FFN, i * 2, False)
            n = 2 * FFN_STEPS
            up_block(4 * B_FFN_LAST, 0, 0, n + 8)
            pe.wait_ge(sem("pair_free0"), n + 10)
            pe.wait_ge(sem("pair_free1"), n + 10)
            pe.wait_ge(sem("p_split"), 2)
            q = 4 * B_PLE_DOWN
            row_quarter(q, q, bank[0:4], (p_hi, p_lo), 0, True, False)
            down_block(4 * B_FFN_LAST, 5, n, False, True, 2)
            row_quarter(q + 3, q + 3, bank[0:4], (p_hi, p_lo), 1, False, True)
            norm_turn(2)
            for i in range(2):
                token_project(B_PLE_GATE + i, 22 + i, norm=None if i else 2)


            pe.wait_ge(sem("constants_loaded"), 16 * N_CONSTANT_LOADS)
            norm_turn(3)
            for t in range(NT):
                for k in range(KD):
                    if t == 0:
                        pe.wait_ge(sem("h_lo_done"), KD * 3 + max(k + 1, 2))
                    c = slice(k * 24, (k + 1) * 24)
                    ins = three(bank[4][:, t * 24:(t + 1) * 24], (sm_hi[:, c], sm_lo[:, c]),
                                [x[:, k, t * P:(t + 1) * P] for x in (h_hi, h_lo)], k == 0, k == KD - 1, False)
            ins.then_inc(sem("small_ready"), 1)

            def rotate(r):
                src = (iq[:, 0:2, :], iq[:, 2:4, :], ik[:, 0:1, :], bk[:, :, :], bq[:, 0:2, :], bq[:, 2:4, :])[r]
                await_read(24 + r // 2)
                if r == 0:
                    pe.wait_ge(sem("small_stored"), 1)
                if r >= 2:
                    pe.wait_ge(sem("rope_added"), 3 * (r - 2) + 1)
                n = S if r == 2 else 512
                mm(bank[6 + r % 2][:, 0:n], con[:, CON["rotate"]], src, start=True, stop=True)\
                    .then_inc(sem("rotated"), 1)

            def index_scores(x):
                t, keys = (0, P) if x == 0 else (1, S)
                heads = range(8) if x == 0 else range(4 * (x - 1), 4 * x)
                if x == 0:
                    pe.wait_ge(sem("rope_added"), 9)
                else:
                    pe.wait_ge(sem("index_relu"), 2 * x)
                for odd in (0, 1):
                    for j, h in enumerate(heads[odd::2]):
                        at = HD * odd
                        ins = mm(bank[4 + odd][:, j * keys:(j + 1) * keys], iq[at:at + HD, h // 2, t * P:(t + 1) * P],
                                 ik[at:at + HD, 0, 0:keys], start=True, stop=True)
                    ins.then_inc(sem("index_scores"), 1)

            def kv_project(b, u):
                await_pair(u)
                for f in range(3):
                    second_beside(4 * (b - B_IQ) + f)
                    feature_quarter(4 * b + f, 4 * b + f, pair(u)[f // 2][:, f % 2 * S:(f % 2 + 1) * S])
                q = 4 * b + 3
                second_beside(4 * (b - B_IQ) + 3)
                await_quarter(q)
                w = [x.rearrange("p (k c) -> p k c", c=P) for x in quarter(q)]
                for t in range(NT):
                    for k in range(KD):
                        ins = three(pair(u)[1][:, S + t * P:S + (t + 1) * P], [x[:, k, :] for x in w],
                                    [x[:, k, t * P:(t + 1) * P] for x in (h_hi, h_lo)], k == 0, k == KD - 1, False)
                ins.then_inc(sem("quarter_done"), 1)

            def second_beside(tick):
                if tick in (6, 7, 10, 11, 13, 14):
                    rotate((6, 7, 10, 11, 13, 14).index(tick))
                if tick in (12, 13, 14):
                    index_scores(tick - 12)
                n = tick - HEAD_TICK
                if 1 <= n <= HEADS:
                    turn_p(HEADS + n - 1)
                if n == 0:
                    pe.wait_ge(sem("masks_ready"), NT)
                    pe.wait_ge(sem("rope_added"), 18)
                if 0 <= n < HEADS:
                    scores(HEADS + n, bq, bk, lambda f: f // 2)
                if 2 <= n < HEADS + 2:
                    head_out(HEADS + n - 2, bv, HD * ((n - 2) // 4))
                if n == HEADS:
                    square_sums()
                if n == HEADS + 1:
                    spread_roots(0)
                    spread_roots(1)
                    pe.wait_ge(sem("head_stored"), 4 * HEADS)
                    mix_turn(4)
                    spread_roots(2)
                    spread_roots(3)
                delta_slot(2 * tick, delta_step)

            def square_sums():
                pe.wait_ge(sem("negated_ready"), 4 * HEADS)
                pe.wait_ge(sem("squared"), 4)
                for t in range(NT):
                    for f in range(8):
                        at = f % 2 * S + t * P
                        ins = mm(bank[4][:, t * 16 + 2 * f:t * 16 + 2 * f + 2], squares[:, f // 2, at:at + P],
                                 con[:, CON["head_sum"]][:, 0:P:HD], start=True, stop=True)
                ins.then_inc(sem("square_sums"), 1)

            def spread_roots(i):
                pe.wait_ge(sem("roots_widened"), i // 2 + 1)
                if i >= 2:
                    pe.wait_ge(sem("qk_normed"), i - 1)
                for f in range(2):
                    for t in range(NT):
                        of = roots_wide[:, t, (4 * i + 2 * f) * HD:(4 * i + 2 * f + 2) * HD]
                        ins = mm(bank[4 + i % 2][:, f * S + t * P:f * S + (t + 1) * P], of, ident, start=True, stop=True)
                ins.then_inc(sem("roots_spread"), 1)

            def delta_prelude(t):
                pe.wait_ge(sem("qk_normed"), 4)
                pe.wait_ge(sem("mix_lo_done"), 12)
                if t:
                    pe.wait_ge(sem("o_stored"), 2 * 2 * t)
                    pe.wait_ge(sem("state_ready"), 2 * 2 * t)
                for dst, src in ((bank[4], ak), (bank[5], av)):
                    for f in range(4):
                        ins = nc.tensor.transpose(dst[:, f * P:(f + 1) * P], src[:, f, t * P:(t + 1) * P], ident)
                g = decay_g[:, t, :]
                pe.wait_ge(sem("g_ready"), 1)
                mm(bank[6][:, 0:8], con[:, CON["tri"]], g, start=True, stop=True)
                mm(bank[6][:, 8:16], con[:, CON["upper"]], g, start=True, stop=True)
                for c in range(2):
                    for odd in range(2):
                        ins = mm(bank[6][HD * odd:HD * (odd + 1), 16 + 4 * c:20 + 4 * c],
                                 con[:, CON["chunk_ones"]][:, c * CHUNK:(c + 1) * CHUNK], g[:, odd::2],
                                 start=True, stop=True)
                ins.then_inc(sem("prelude_ready"), 1)

            def delta_stage(t, stage, g):
                d, first, second = delta[g], 4 + 2 * g, 5 + 2 * g
                at = HD * g
                if stage:
                    pe.wait_ge(sem(f"delta_scalar{g}"), DELTA_SCALAR[-1] * t + DELTA_SCALAR[stage - 1])
                    pe.wait_ge(sem(f"delta_vector{g}"), DELTA_VECTOR[-1] * t + DELTA_VECTOR[stage - 1])

                def each(b, column, lhs, rhs):
                    c = rhs.shape[2]
                    for m in range(4):
                        ins = mm(bank[b][:, column + m * c:column + (m + 1) * c], lhs[:, m, :], rhs[:, m, :],
                                 start=True, stop=True)
                    return ins

                if stage == 0:
                    pe.wait_ge(sem("g_masked_ready"), 2 * (t + 1))
                    pe.wait_ge(sem("r_ready"), 3 * (t + 1))
                    pe.wait_ge(sem("exp_g_ready"), t + 1)
                    mm(bank[first][:, 0:S], con[:, CON["tri"]], g_upper[:, g::2, :], start=True, stop=True)
                    mm(bank[first][:, S:512], con[:, CON["upper"]], g_tri[:, g::2, :], start=True, stop=True)
                    for column, other in ((0, ak), (S, aq)):
                        for c in range(2):
                            chunk = slice(t * P + c * CHUNK, t * P + (c + 1) * CHUNK)
                            for m in range(4):
                                ins = mm(bank[second][c * CHUNK:(c + 1) * CHUNK, column + m * CHUNK:column + (m + 1) * CHUNK],
                                         ak[at:at + HD, m, chunk], other[at:at + HD, m, chunk], start=True, stop=True)
                elif stage == 1:
                    for m in range(4):
                        ins = nc.tensor.transpose(bank[first][:, m * P:(m + 1) * P], d["near_d"][:, m, :], ident)
                elif stage == 2:
                    each(first, 0, d["near_td"], d["near_c"])
                    ins = each(second, 0, d["near_d"], d["near_tc"])
                elif stage == 3:
                    sq_td = d["inv_td"]
                    each(first, 0, sq_td, d["sq_c"])
                    each(second, S, d["sq_d"], d["sq_tc"])
                    ins = each(second, 0, d["sq_d"], d["inv_tc"])
                elif stage == 4:
                    each(first, 0, d["near_td"], d["near_c"])
                    ins = each(second, 0, d["near_d"], d["inv_tc"])
                elif stage == 5:
                    ins = each(second, 0, d["sq_d"], d["inv_tc"])
                elif stage == 6:
                    each(first, 0, d["inv_td"], d["far_c"])
                    each(first, S, d["far_d"], d["inv_tc"])
                    ins = each(second, 0, d["inv_td"], r_sb[:, g::2, :])
                elif stage == 7:
                    ins = each(first, 0, d["near_d"], d["near_tc"])
                elif stage == 8:
                    ins = each(second, 0, d["sq_d"], d["y"])
                else:
                    each(second, 0, d["far_d"], d["y"][:, :, 0:HD])
                    for m in range(4):
                        ins = mm(bank[first][at:at + HD, m * P:(m + 1) * P], d["y"][:, m, HD:P], d["far_d"][:, m, :],
                                 start=True, stop=True)
                ins.then_inc(sem(f"delta_ready{g}"), 1)

            def old_state(c):
                t, r0 = c // 2, CHUNK * (c % 2)
                rows = slice(r0, r0 + CHUNK)
                for g in range(2):
                    at = HD * g
                    pe.wait_ge(sem(f"delta_scalar{g}"), DELTA_SCALAR[-1] * (t + 1))
                    pe.wait_ge(sem(f"delta_vector{g}"), DELTA_VECTOR[-1] * (t + 1))
                    pe.wait_ge(sem("state_ready"), 2 * (c - 1) + g + 1)
                    pe.wait_ge(sem("o_stored"), 2 * (c - 1) + g + 1)
                    for column, lhs, l0 in ((0, w_t, r0), (S, aq, t * P + r0)):
                        for m in range(4):
                            ins = mm(bank[4 + 2 * g][rows, column + m * HD:column + (m + 1) * HD],
                                     lhs[at:at + HD, m, l0:l0 + CHUNK], state[at:at + HD, m * HD:(m + 1) * HD],
                                     start=True, stop=True)
                    ins.then_inc(sem("state_used"), 1)

            def new_values(c):
                r0 = CHUNK * (c % 2)
                rows = slice(r0, r0 + CHUNK)
                for g in range(2):
                    at = HD * g
                    pe.wait_ge(sem("v_new_ready"), 2 * c + g + 1)
                    for m in range(4):
                        mm(bank[5 + 2 * g][rows, m * HD:(m + 1) * HD], qk_t[rows, g, m, :],
                           v_new[rows, g, m * HD:(m + 1) * HD], start=True, stop=True)
                    for m in range(4):
                        ins = mm(bank[5 + 2 * g][at:at + HD, S + m * HD:S + (m + 1) * HD], k_dec[rows, 2 * m + g, :],
                                 v_new[rows, g, m * HD:(m + 1) * HD], start=True, stop=True)
                    ins.then_inc(sem("v_new_used"), 1)

            def delta_step(kind, n, stage=None):
                if kind == "begin":
                    delta_prelude(n)
                elif kind == "stage":
                    for g in range(2):
                        delta_stage(n, stage, g)
                elif kind == "old":
                    old_state(n)
                else:
                    new_values(n)

            def beside(block_):
                first = 4 * (block_ - B_IQ)
                return {"beside": lambda f: second_beside(first + f)}

            def with_middle(block_):
                first = 4 * (block_ - B_IQ)
                return beside(block_) | {"middle": lambda f: delta_slot(2 * (first + f) + 1, delta_step)}

            feature_project(B_IQ, 24)
            kv_project(B_KV, 25)
            feature_project(B_BQ, 26, **with_middle(B_BQ))
            for i in range(3):
                feature_project(B_AQ + i, 27 + i, **with_middle(B_AQ + i))
            token_project(B_AZ, 30, **beside(B_AZ))
            for i in range(4):
                feature_project(B_GATES + i, 31 + i, **with_middle(B_GATES + i))
            for i in range(2):
                for f in range(4):
                    q = 4 * (B_PROJ + i) + f
                    second_beside(q - 4 * B_IQ)
                    if i == 1 and f == 0:
                        pe.wait_ge(sem("o_gated"), NT)
                        mix_turn(0)
                    u = 35 + 2 * i + f // 2
                    if f % 2 == 0:
                        await_pair(u)
                    if f == 0:
                        pe.wait_ge(sem("mix_lo_done"), 12 + 4 * i)
                    await_quarter(q)
                    w = [x.rearrange("p (f k c) -> p f k c", f=2, c=P) for x in quarter(q)]
                    for j in range(2):
                        if j:
                            delta_slot(2 * (q - 4 * B_IQ) + 1, delta_step)
                        for k in range(4):
                            ins = three(pair(u)[f % 2][:, j * S:(j + 1) * S], [x[:, j, k, :] for x in w],
                                        [x[:, 4 * (1 - i) + k, :] for x in (g_hi, g_lo)], k == 0, k == 3, True)
                    ins.then_inc(sem("quarter_done"), 1)
            for n, (c, f) in enumerate(WOUT2_ORDER):
                if f == 0:
                    await_pair(39 + c)
                pe.wait_ge(sem("merged_lo_done"), f + 1)
                token_quarter(4 * B_WOUT2 + n, 39 + c, f, (h_hi, h_lo))
            norm_turn(4)
            for t in range(NT):
                for k in range(KD):
                    if t == 0:
                        pe.wait_ge(sem("h_lo_done"), KD * 4 + max(k + 1, 2))
                    c = slice(KD * 24 + k * 20, KD * 24 + (k + 1) * 20)
                    ins = three(bank[4][:, t * 20:(t + 1) * 20], (sm_hi[:, c], sm_lo[:, c]),
                                [x[:, k, t * P:(t + 1) * P] for x in (h_hi, h_lo)], k == 0, k == KD - 1, False)
            ins.then_inc(sem("logits_ready"), 1)

            def expert_up(base, q0, i, free):
                pe.wait_ge(sem(f"pair_free{1 - i}"), free)
                for f in range(4):
                    feature_quarter(base + q0 + f, q0 + f, pair(1 - i)[f // 2][:, f % 2 * S:(f % 2 + 1) * S])

            def expert_down(base, q0, n, start, stop):
                for k in range(4):
                    if k % 2 == 0:
                        pe.wait_ge(sem("expert_lo_done"), n + k // 2 + 1)
                    row_quarter(base + q0 + k, q0 + k, bank[4:8], (g_hi, g_lo), k, start and k == 0, stop and k == 3)

            off = 4 * B_MOE % RING
            base = 4 * B_MOE - off
            expert_up(base, off, 0, 40)
            expert_up(base, off + 4, 1, 42)
            pe.wait_ge(sem("comb_ready"), NT)
            for t in range(NT):
                ins = nc.tensor.transpose(bank[4][0:N_EXPERTS, t * P:(t + 1) * P], comb[:, t, :], ident)
            ins.then_inc(sem("comb_turned"), 1)
            pe.wait_ge(sem("comb_t_stored"), 1)
            pe.wait_ge(sem("selectors_loaded"), 16)
            for e in range(0, N_EXPERTS, 2):
                if e >= 6:
                    pe.wait_ge(sem("comb_stored"), e // 2 - 2)
                for j in range(2):
                    ins = mm(bank[5 + e // 2 % 3][:, j * S:(j + 1) * S], selectors[0:N_EXPERTS, (e + j) * P:(e + j + 1) * P],
                             comb_t, start=True, stop=True)
                ins.then_inc(sem("comb_spread"), 1)
            pe.wait_ge(sem("comb_stored"), N_EXPERTS // 2)
            expert_down(base, off + 8, 0, True, False)
            with pe.Fori(1, MOE_STEPS - 1) as i:
                expert_up(i * 12 + base, off, 0, i * 2 + 40)
                expert_up(i * 12 + base, off + 4, 1, i * 2 + 42)
                expert_down(i * 12 + base, off + 8, i * 2, False, False)
            n = 2 * (MOE_STEPS - 1)
            last = base + 12 * (MOE_STEPS - 1)
            expert_up(last, off, 0, n + 40)
            expert_up(last, off + 4, 1, n + 42)
            expert_down(last, off + 8, n, False, True)

        @block.vector
        def _(dve):
            V = nc.vector
            chain = [0]

            def link(ins):
                chain[0] += 1
                ins.then_inc(sem("vector_link"), 1)
                dve.wait_ge(sem("vector_link"), chain[0])

            def rsqrt(y, v_, t):
                link(V.tensor_scalar(t.bitcast(I32), v_.bitcast(I32), 1, None, ALU.logical_shift_right))
                link(V.tensor_scalar(y.bitcast(I32), t.bitcast(I32), -1.0, float(RSQRT_SEED), ALU.mult, ALU.add))
                for _ in range(3):
                    link(V.tensor_tensor(t, y, y, ALU.mult))
                    link(V.scalar_tensor_tensor(t, t, -0.5, v_, ALU.mult, ALU.mult))
                    link(V.scalar_tensor_tensor(y, t, 1.5, y, ALU.add, ALU.mult))

            def norm(n=None):
                link(V.tensor_tensor_reduce(tok3[:, 0, :], x3[:, 0, :], x3[:, 0, :], 1.0 / D, 0.0, ALU.mult, ALU.add,
                                            stat[:, 0:1]))
                norm.count += 1
                dve.wait_ge(sem("second_squares"), norm.count)
                link(V.tensor_scalar(stat[:, 2:4], stat[:, 0:2], RMS_EPS, None, ALU.add))
                rsqrt(stat[:, 4:6], stat[:, 2:4], stat[:, 6:8])
                if n is not None:
                    for t in range(NT):
                        V.tensor_scalar(tok3[:, t, :], x3[:, t, :], stat[:, 4 + t:5 + t], None, ALU.mult)\
                            .then_inc(sem("x_normed"), 1)

            norm.count = 0

            def norm_lo(n, gain):
                for k in range(KD):
                    dve.wait_ge(sem("h_hi_done"), KD * n + k // 2 * 2 + 2)
                    V.scalar_tensor_tensor(h_lo[:, k, :], bank[4 + k // 2][:, k % 2 * S:(k % 2 + 1) * S], v(gain, k),
                                           h_hi[:, k, :].bitcast(F32), ALU.mult, ALU.subtract)\
                        .then_inc(sem("h_lo_done"), 1)

            def store_pair(b, u, dsts):
                for i, dst in enumerate(dsts):
                    dve.wait_ge(sem("quarter_done"), 4 * b + 4)
                    V.tensor_copy(dst, pair(u)[i][:, :]).then_inc(sem(f"pair_free{u % 2}"), 1)

            def halves(a):
                return a[:, 0:2, :], a[:, 2:4, :]

            def negate(n, mask):
                dve.wait_ge(sem("scores_ready"), n + 1)
                if n >= 2:
                    dve.wait_ge(sem("p_turned"), n - 1)
                p = moba_p[:, n % 2 * 384:(n % 2 + 1) * 384]
                for t, part in ((0, slice(0, P)), (1, slice(P, 384))):
                    i = 2 * (n % HEADS) + t
                    V.tensor_tensor_reduce(p[:, part], bank[4 + n % 2][:, part], mask(t), -HD ** -0.5, 3e38,
                                           ALU.add, ALU.min, stat[:, 32 + i:33 + i]).then_inc(sem("negated_ready"), 1)

            def store_head(n, at):
                dve.wait_ge(sem("head_out"), n + 1)
                i = 2 * (n % HEADS)
                link(V.reciprocal(stat[:, 48 + i:50 + i], stat[:, 48 + i:50 + i]))
                for t in range(NT):
                    V.tensor_scalar(tok3[:, t, at:at + HD], bank[6 + n % 2][:, 384 + HD * t:448 + HD * t],
                                    stat[:, 48 + i + t:49 + i + t], None, ALU.mult).then_inc(sem("head_stored"), 1)

            def ret_decay(h):
                dve.wait_ge(sem("ret_scores"), h + 1)
                if h >= 2:
                    dve.wait_ge(sem("ret_out"), h - 1)
                s, d = ret_s[:, h % 2 * 384:(h % 2 + 1) * 384], decay[:, h * S:(h + 1) * S]
                V.tensor_tensor(s[:, 0:S], bank[4 + h % 2][:, 0:S], d, ALU.mult).then_inc(sem("ret_s_ready"), 1)
                V.tensor_tensor(s[:, S:384], bank[4 + h % 2][:, S:384], d[:, 0:P], ALU.mult)\
                    .then_inc(sem("ret_s_ready"), 1)

            dve.wait_ge(sem("x_loaded"), 16 * NT)
            norm(0)
            dve.wait_ge(sem("first_constants"), 32)
            norm_lo(0, "attn_norm")
            dve.wait_ge(sem("constants_loaded"), 16 * N_CONSTANT_LOADS)
            for h in range(HEADS):
                V.tensor_scalar(bias[:, h, :], dist, -(HD ** 0.5) * 2.0 ** (-8.0 * (h + 1) / HEADS), None,
                                ALU.mult).then_inc(sem("bias_ready"), 1)
            store_pair(B_MQ, 0, halves(mq))
            store_pair(B_MK, 1, halves(mk))
            for hi_, lo_, src in ((p_hi, p_lo, p_raw.rearrange("p (k s) -> p k s", s=S)),
                                  (sm_hi[:, :], sm_lo[:, :], small_raw[:, :])):
                link(V.tensor_copy(hi_, src))
                V.tensor_tensor(lo_, src, hi_.bitcast(F32), ALU.subtract).then_inc(sem("p_split"), 1)
            dve.wait_ge(sem("positions_loaded"), 16)
            link(V.tensor_copy(angle, turns.bitcast(I32)))
            link(V.tensor_scalar(angle, angle, v("inv_freq"), None, ALU.mult))
            for dst, shift in ((sin, 0.0), (cos, 0.25)):
                link(V.tensor_scalar(dst, angle, 1 / (2 * np.pi), shift, ALU.mult, ALU.add))
                link(V.tensor_scalar(dst, dst, ROUND, -ROUND, ALU.add, ALU.add))
            for dst, whole, shift in ((turns, sin, 0.0), (angle, cos, np.pi / 2)):
                link(V.scalar_tensor_tensor(dst, whole, -TWO_PI[0], angle, ALU.mult, ALU.add))
                link(V.scalar_tensor_tensor(dst, whole, -TWO_PI[1], dst, ALU.mult, ALU.add))
                link(V.scalar_tensor_tensor(dst, whole, -TWO_PI[2], dst, ALU.mult, ALU.add))
                if shift:
                    link(V.tensor_scalar(dst, dst, shift, None, ALU.add))
                V.tensor_scalar(dst, dst, 3.1415925, -3.1415925, ALU.min, ALU.max).then_inc(sem("angles_ready"), 1)
            V.tensor_scalar(gate_bias[:, :], v("b_gate", 0, 2 * KD), 0.5, None, ALU.mult).then_inc(sem("gate_bias_ready"), 1)
            V.memset(root_bias[:, 0:1], HD * 4 * RMS_EPS)
            V.memset(root_bias[:, 1:2], 4 * RMS_EPS).then_inc(sem("root_bias_ready"), 1)
            dve.wait_ge(sem("bias_ready"), HEADS)
            for tick in range(16):
                if tick == 2:
                    store_pair(B_MV, 2, (mv[:, 0, :], mv[:, 1, :]))
                if tick < HEADS:
                    negate(tick, lambda t: bias[:, tick, P - t * P:S])
                if 2 <= tick < HEADS + 2:
                    store_head(tick - 2, HD * (tick - 2))
                if tick == 4:
                    store_pair(B_RQ, 3, halves(rq))
                if tick == 8:
                    store_pair(B_RK, 4, halves(rk))
                if tick in (10, 11):
                    ret_decay(tick - 10)
                if tick == 12:
                    store_pair(B_RV, 5, (rv[:, 0, :], rv[:, 1, :]))
                if tick in (13, 14):
                    ret_decay(tick - 11)

            def mix_lo(k, n, gain=None):
                dve.wait_ge(sem("mix_hi_done"), n // 2 * 2 + 2)
                src, hi_ = bank[4 + k // 2][:, (k % 2) * S:(k % 2 + 1) * S], g_hi[:, k, :].bitcast(F32)
                if gain is None:
                    ins = V.tensor_tensor(g_lo[:, k, :], src, hi_, ALU.subtract)
                else:
                    ins = V.scalar_tensor_tensor(g_lo[:, k, :], src, gain, hi_, ALU.mult, ALU.subtract)
                ins.then_inc(sem("mix_lo_done"), 1)

            for k in range(4):
                mix_lo(k, k)
            for t in range(NT):
                dve.wait_ge(sem("rg_tanh_ready"), t + 1)
                V.scalar_tensor_tensor(rg[:, t, :], rg_tanh[:, t, :], 1.0, pair(6)[t][:, :], ALU.add, ALU.mult)\
                    .then_inc(sem("pair_free0"), 1)
            bn = stat[:, 64:112].rearrange("p (g s) -> p g s", s=6)
            agg = stat[:, 112:128].rearrange("p (g s) -> p g s", s=2)
            for h in range(RET_HEADS):
                dve.wait_ge(sem("ret_out"), h // 2 * 2 + 2)
                for t in range(NT):
                    o = bank[6 + h // 2][:, h % 2 * S + t * P:h % 2 * S + (t + 1) * P]
                    V.bn_stats(bn[:, 2 * h + t, :], o).then_inc(sem("bn_stats"), 1)
            for g in range(8):
                dve.wait_ge(sem("bn_stats"), g + 1)
                ins = V.bn_aggr(agg[:, g, :], bn[:, g, :])
                if g < 7:
                    ins.then_inc(sem("bn_aggr"), 1)
            link(ins)
            link(V.tensor_scalar(stat[:, 128:136], agg[:, :, 1], GN_EPS, None, ALU.add))
            rsqrt(stat[:, 136:144], stat[:, 128:136], stat[:, 144:152])
            for g in range(8):
                h, t = g // 2, g % 2
                o = bank[6 + h // 2][:, h % 2 * S + t * P:h % 2 * S + (t + 1) * P]
                ins = V.tensor_scalar(tok3[:, t, 512 + h * P:512 + (h + 1) * P], o, agg[:, g, 0:1],
                                      stat[:, 136 + g:137 + g], ALU.subtract, ALU.mult)
            link(ins)
            dve.wait_ge(sem("pair_free0"), 8)
            for t in range(NT):
                V.scalar_tensor_tensor(tok3[:, t, 512:D], tok3[:, t, 512:D], 0.5, rg[:, t, :], ALU.mult, ALU.mult)\
                    .then_inc(sem("ret_gated"), 1)
            for k in range(4, 8):
                mix_lo(k, k, v("ret_norm", k - 4))

            def add_pair(done, u, c):
                for t in range(NT):
                    dve.wait_ge(sem("quarter_done"), done)
                    V.tensor_tensor(x3[:, t, c * 512:(c + 1) * 512], pair(u)[t][:, :], x3[:, t, c * 512:(c + 1) * 512],
                                    ALU.add).then_inc(sem(f"pair_free{u % 2}"), 1)

            for c in range(2):
                add_pair(4 * B_WOUT + WOUT_ORDER.index((c, 3)) + 1, 7 + c, c)
            dve.wait_ge(sem("pair_free1"), 8)
            dve.wait_ge(sem("pair_free0"), 10)
            norm(1)
            norm_lo(1, "ffn_norm")

            def fvec(name, i):
                return vec[:, bass.ds(i + VEC[name].start, 1)]

            pair_u = [pair(1), pair(0)]

            def ffn_up(b, i, n_up, f):
                for back in (1, 2):
                    if back == 2:
                        dve.wait_ge(sem("conv_step"), n_up * 2 + 2)
                    for j in range(2):
                        if back == 1:
                            dve.wait_ge(sem("conv_first"), n_up * 2 + 2)
                        c, u = conv[:, i, j, back:S], pair_u[i][0][:, j * S:(j + 1) * S - back]
                        ins = V.scalar_tensor_tensor(c, u, fvec("conv_w", (f + j) * 3 + 2 - back), c, ALU.mult, ALU.add)
                        if back == 1:
                            ins.then_inc(sem("conv_step"), 1)
                ins.then_inc(sem(f"pair_free{1 - i}"), 1)
                dve.wait_ge(sem("gelu_done"), n_up + 1)
                dve.wait_ge(sem("quarter_done"), b + 4)
                V.tensor_tensor(act[:, i, :], act[:, i, :], pair_u[i][1][:, :], ALU.mult)\
                    .then_inc(sem(f"pair_free{1 - i}"), 1)
                dve.wait_ge(sem("act_hi_done"), n_up + 1)
                V.tensor_tensor(g_lo[:, 2 * i:2 * i + 2, :], act[:, i, :].rearrange("p (f s) -> p f s", s=S),
                                g_hi[:, 2 * i:2 * i + 2, :].bitcast(F32), ALU.subtract).then_inc(sem("act_lo_done"), 1)

            b = 4 * B_FFN
            ffn_up(b, 0, 0, 0)
            ffn_up(b + 4, 1, 1, 2)
            with dve.Fori(1, FFN_STEPS) as i:
                ffn_up(i * 12 + b, 0, i * 2, i * 4)
                ffn_up(i * 12 + (b + 4), 1, i * 2 + 1, i * 4 + 2)
            ffn_up(4 * B_FFN_LAST, 0, 2 * FFN_STEPS, 4 * FFN_STEPS)
            for t in range(NT):
                for c in range(2):
                    dve.wait_ge(sem("quarter_done"), 4 * B_PLE_DOWN + 3)
                    part = x3[:, t, c * 512:(c + 1) * 512]
                    V.tensor_tensor(part, bank[4 + 2 * t + c][:, :], part, ALU.add).then_inc(sem("x_summed"), 1)
            dve.wait_ge(sem("x_summed"), 4)
            norm(2)
            for t in range(NT):
                for c in range(2):
                    dve.wait_ge(sem("quarter_done"), 4 * B_PLE_DOWN + 4)
                    V.tensor_copy(ple3[:, t, c * 512:(c + 1) * 512], bank[2 * t + c][:, :])\
                        .then_inc(sem(f"pair_free{t}"), 1)
            norm_lo(2, "ple_norm")
            for c in range(2):
                for t in range(NT):
                    dve.wait_ge(sem(f"pair_free{c}"), 22 + t + 1)
                    link(V.scalar_tensor_tensor(ple_tanh[:, t, :], ple_tanh[:, t, :], 1.0,
                                                ple3[:, t, c * 512:(c + 1) * 512], ALU.add, ALU.mult))
                    part = x3[:, t, c * 512:(c + 1) * 512]
                    V.scalar_tensor_tensor(part, ple_tanh[:, t, :], 0.5, part, ALU.mult, ALU.add)\
                        .then_inc(sem("ple_added"), 1)
            dve.wait_ge(sem("ple_added"), 2 * NT)
            norm()
            dve.wait_ge(sem("norm_row_loaded"), 16)
            for t in range(NT):
                V.scalar_tensor_tensor(x3[:, t, :], x3[:, t, :], stat[:, 4 + t:5 + t], norm_row, ALU.mult, ALU.mult)\
                    .then_inc(sem("first_out"), 1)

            dve.wait_ge(sem("first_out"), NT)
            norm(3)
            norm_lo(3, "norm1")

            def spread(column, n):
                return column.unsqueeze(2).broadcast_to([column.shape[0], column.shape[1], n])

            def each_of(a, n):
                return a.unsqueeze(1).broadcast_to([a.shape[0], n, a.shape[1]])

            dve.wait_ge(sem("small_ready"), 1)
            V.tensor_copy(small_tok, bank[4][:, 0:NT * 24].rearrange("p (t n) -> p t n", t=NT))\
                .then_inc(sem("small_stored"), 1)
            dve.wait_ge(sem("small_stored"), 1)
            V.tensor_scalar(index_w, small_tok[:, :, 16:24], HEADS ** -0.5 * HD ** -0.5, None, ALU.mult)\
                .then_inc(sem("index_w_ready"), 1)
            link(V.tensor_tensor(soft_a, small_tok[:, :, 8:16], each_of(row[:, ROW["dt_bias"]], NT), ALU.add))
            V.scalar_tensor_tensor(soft_b, soft_a, -1.0, soft_a, ALU.mult, ALU.min).then_inc(sem("soft_in_ready"), 1)
            dve.wait_ge(sem("soft_ready"), 1)
            link(V.tensor_scalar(beta, beta, 0.5, 0.5, ALU.mult, ALU.add))
            V.tensor_scalar(beta_half, beta, 0.5, None, ALU.mult).then_inc(sem("beta_ready"), 1)
            link(V.scalar_tensor_tensor(decay_g, soft_a, 0.0, soft_b, ALU.max, ALU.add))
            link(V.tensor_scalar(decay_g, decay_g, -1.0, None, ALU.mult))
            V.tensor_tensor(decay_g, decay_g, each_of(rate[:, :], NT), ALU.mult).then_inc(sem("g_ready"), 1)

            def rope(r):
                x = (iq[:, 0:2, :], iq[:, 2:4, :], ik[:, 0:1, :], bk[:, :, :], bq[:, 0:2, :], bq[:, 2:4, :])[r]
                n = x.shape[1]
                dve.wait_ge(sem("rotated"), r + 1)
                tmp = rope_tmp[:, r % 2, 0:n * S].rearrange("p (f s) -> p f s", s=S)
                turned = bank[6 + r % 2][:, 0:n * S].rearrange("p (f s) -> p f s", s=S)
                V.tensor_tensor(tmp, turned, each_of(sin, n), ALU.mult).then_inc(sem("rope_added"), 1)
                V.tensor_tensor(x, x, each_of(cos, n), ALU.mult).then_inc(sem("rope_added"), 1)
                dve.wait_ge(sem("rope_added"), 3 * r + 2)
                V.tensor_tensor(x, x, tmp, ALU.add).then_inc(sem("rope_added"), 1)

            def conv2(n, dst):
                u = 27 + n
                dve.wait_ge(sem("conv2_first"), 4 * n + 4)
                for back in (1, 2, 3):
                    for f in range(4):
                        if back > 1:
                            dve.wait_ge(sem("conv2_step"), 8 * n + 4 * (back - 2) + f + 1)
                        c = dst[:, f, back:S]
                        src = pair(u)[f // 2][:, f % 2 * S:(f % 2 + 1) * S - back]
                        ins = V.scalar_tensor_tensor(c, src, v("conv_w2", (4 * n + f) * 4 + 3 - back), c, ALU.mult, ALU.add)
                        if back < 3:
                            ins.then_inc(sem("conv2_step"), 1)
                        elif f % 2:
                            ins.then_inc(sem(f"pair_free{u % 2}"), 1)

            def silu2(n, dst):
                for i in range(2):
                    dve.wait_ge(sem("silu_tanh_ready"), 2 * n + i + 1)
                    x = dst[:, 2 * i:2 * i + 2, :]
                    V.scalar_tensor_tensor(x, silu_tanh[:, i, :].rearrange("p (f s) -> p f s", s=S), 1.0, x,
                                           ALU.add, ALU.mult).then_inc(sem("silu_done"), 1)

            added = [0]

            def index_add(x):
                t, keys = (0, P) if x == 0 else (1, S)
                heads = range(8) if x == 0 else range(4 * (x - 1), 4 * x)
                acc = index[:, t, 0:keys]
                for odd in range(2):
                    dve.wait_ge(sem("index_relu"), 2 * x + odd + 1)
                    for j, h in enumerate(heads[odd::2]):
                        src, w = relu[:, odd, j * keys:(j + 1) * keys], index_w[:, t, h:h + 1]
                        if x < 2 and j == odd == 0:
                            dve.wait_ge(sem("index_w_ready"), 1)
                            ins = V.tensor_scalar(acc, src, w, None, ALU.mult)
                        else:
                            dve.wait_ge(sem("index_added"), added[0])
                            ins = V.scalar_tensor_tensor(acc, src, w, acc, ALU.mult, ALU.add)
                        ins.then_inc(sem("index_added"), 1)
                        added[0] += 1

            def choose_keys():
                tiles = [(index[:, t, 0:(t + 1) * P], best[:, 8 * t:8 * t + 8]) for t in range(NT)]
                rounds = [0]

                def step(make):
                    for t, (acc, eight) in enumerate(tiles):
                        if rounds[0]:
                            dve.wait_ge(sem("keys_chosen"), 2 * rounds[0] - 1 + t)
                        make(t, acc, eight).then_inc(sem("keys_chosen"), 1)
                    rounds[0] += 1

                dve.wait_ge(sem("index_added"), 16)

                def limit(t, acc, eight):
                    part = acc[:, t * P:(t + 1) * P]
                    return V.tensor_tensor(part, part, con[:, CON["key_limit"]], ALU.add)

                step(limit)
                for _ in range(TOPK // 8):
                    step(lambda t, acc, eight: V.max(eight, acc))
                    step(lambda t, acc, eight: V.match_replace(acc, eight, acc, -3e38))
                dve.wait_ge(sem("keys_chosen"), 2 * rounds[0])
                for t, (acc, _) in enumerate(tiles):
                    V.tensor_scalar(masks[:, t, 0:(t + 1) * P], acc, -2e38, -1e31, ALU.is_gt, ALU.mult)\
                        .then_inc(sem("masks_ready"), 1)

            dve.wait_ge(sem("rope_tables"), 1)
            for r in range(4):
                rope(r)
            index_add(0)
            rope(4)
            index_add(1)
            rope(5)
            index_add(2)
            choose_keys()
            conv2(0, aq)
            silu2(0, aq)
            dve.wait_ge(sem("masks_ready"), NT)
            for k in range(HEADS + 2):
                if k < HEADS:
                    negate(HEADS + k, lambda t: masks[:, t, 0:(t + 1) * P])
                if k == 1:
                    conv2(1, ak)
                if k == 4:
                    silu2(1, ak)
                if k == HEADS + 1:
                    dve.wait_ge(sem("rooted"), 2)
                    link(V.reciprocal(roots, roots))
                    for i in range(2):
                        V.tensor_copy(roots_wide[:, :, 512 * i:512 * (i + 1)].rearrange("p t (h c) -> p t h c", c=HD),
                                      roots[:, :, 8 * i:8 * i + 8].unsqueeze(3).broadcast_to([P, NT, 8, HD]))\
                            .then_inc(sem("roots_widened"), 1)
                if k >= 2:
                    store_head(HEADS + k - 2, 512 + HD * (k - 2))
                if k == 5:
                    conv2(2, av)
                if k == 8:
                    silu2(2, av)
            for i in range(4):
                dve.wait_ge(sem("roots_spread"), i + 1)
                x = (aq, ak)[i // 2][:, 2 * (i % 2):2 * (i % 2) + 2, :]
                V.tensor_tensor(x, x, bank[4 + i % 2][:, :].rearrange("p (f s) -> p f s", s=S), ALU.mult)\
                    .then_inc(sem("qk_normed"), 1)
            for k in range(4, 8):
                mix_lo(k, 4 + k)
            for t in range(NT):
                dve.wait_ge(sem("az_tanh_ready"), t + 1)
                V.scalar_tensor_tensor(az[:, t, :], tok3[:, t, 0:512], 1.0, pair(30)[t][:, :], ALU.add, ALU.mult)\
                    .then_inc(sem("pair_free0"), 1)
            def delta_begin(t):
                if t:
                    dve.wait_ge(sem("v_new_used"), 4)
                    dve.wait_ge(sem("o_stored"), 4)
                dve.wait_ge(sem("g_ready"), 1)
                for dst, mask in ((g_upper, "upper_c"), (g_tri, "tri_c")):
                    V.tensor_tensor(dst, each_of(con[:, CON[mask]], HEADS), spread(decay_g[:, t, :], CHUNK), ALU.mult)\
                        .then_inc(sem("g_masked_ready"), 1)
                dve.wait_ge(sem("prelude_ready"), t + 1)
                dve.wait_ge(sem("exp_g_ready"), t + 1)
                link(V.tensor_tensor(beta_g[:, :], beta[:, t, :], exp_g[:, 0:8], ALU.mult))
                k, val = (b[:, :].rearrange("p (h c) -> p h c", c=HD) for b in (bank[4], bank[5]))
                dve.wait_ge(sem("beta_ready"), 1)
                V.tensor_tensor(r_sb[:, :, 0:HD], val, spread(beta_half[:, t, :], HD), ALU.mult).then_inc(sem("r_ready"), 1)
                V.tensor_tensor(r_sb[:, :, HD:P], k, spread(beta_g[:, :], HD), ALU.mult).then_inc(sem("r_ready"), 1)
                V.tensor_tensor(k_dec, k, spread(exp_g[:, 8:16], HD), ALU.mult).then_inc(sem("r_ready"), 1)

            def delta_stage(t, stage, g):
                d, b, done = delta[g], 5 + 2 * g, sem(f"delta_vector{g}")
                was = DELTA_VECTOR[-1] * t
                first, second, whole = bank_part(b, 0, CHUNK), bank_part(b, S, CHUNK), bank_part(b, 0, P)
                identity = con[:, CON["ident_c"]]
                if stage != 7:
                    dve.wait_ge(sem(f"delta_ready{g}"), 10 * t + stage + 1)

                def made(ins):
                    ins.then_inc(done, 1)

                def to_diagonal(name, x, y=None, how=None):
                    for c in range(2):
                        dst = halves_of(d[name], c)
                        if y is None:
                            made(V.tensor_copy(dst, halves_of(x, c)))
                        else:
                            made(V.tensor_tensor(dst, halves_of(x, c), halves_of(y, c), how))

                if stage == 0:
                    dve.wait_ge(sem(f"delta_scalar{g}"), DELTA_SCALAR[-1] * t + 2)
                    qk = qk_t[:, g, :, :]
                    made(V.tensor_tensor(d["far_c"], first, d["near_tc"], ALU.mult))
                    made(V.tensor_tensor(qk, second, d["inv_tc"], ALU.mult))
                    dve.wait_ge(done, was + 1)
                    made(V.tensor_tensor(d["far_c"], d["far_c"], spread(beta[:, t, g::2], CHUNK), ALU.mult))
                    dve.wait_ge(done, was + 2)
                    made(V.tensor_tensor(qk, qk, each_of(con[:, CON["tri_c"]], 4), ALU.mult))
                    dve.wait_ge(done, was + 3)
                    near = each_of(con[:, CON["near_c"]], 4)
                    made(V.tensor_tensor(d["near_c"], d["far_c"], near, ALU.mult))
                    to_diagonal("near_d", d["far_c"], near, ALU.mult)
                elif stage == 1:
                    dve.wait_ge(sem(f"delta_scalar{g}"), DELTA_SCALAR[-1] * t + DELTA_SCALAR[1])
                    made(V.tensor_tensor(d["inv_tc"], each_of(identity, 4), d["near_tc"], ALU.subtract))
                elif stage == 2:
                    made(V.tensor_copy(d["sq_tc"], first))
                    to_diagonal("inv_td", first)
                elif stage == 3:
                    to_diagonal("near_td", second)
                    made(V.tensor_tensor(d["inv_tc"], first, d["inv_tc"], ALU.add))
                elif stage == 4:
                    made(V.tensor_tensor(d["inv_tc"], first, d["inv_tc"], ALU.add))
                    far = each_of(con[:, CON["far_c"]], 4)
                    to_diagonal("far_d", d["far_c"], far, ALU.mult)
                    dve.wait_ge(done, was + DELTA_VECTOR[4] - 1)
                    made(V.tensor_tensor(d["far_c"], d["far_c"], far, ALU.mult))
                elif stage == 5:
                    to_diagonal("inv_td", first, d["inv_tc"], ALU.add)
                    dve.wait_ge(done, was + DELTA_VECTOR[5] - 1)
                    made(V.tensor_tensor(d["inv_tc"], first, d["inv_tc"], ALU.add))
                elif stage == 6:
                    made(V.tensor_copy(d["y"], whole))
                elif stage == 7:
                    dve.wait_ge(sem(f"delta_scalar{g}"), DELTA_SCALAR[-1] * t + DELTA_SCALAR[6])
                    to_diagonal("far_d", each_of(identity, 4), d["near_tc"], ALU.subtract)
                elif stage == 8:
                    made(V.tensor_tensor(d["y"], whole, d["y"], ALU.add))
                else:
                    made(V.tensor_copy(u_sb[:, g, :], bank[b][:, 0:S]))

            def values(c):
                r0 = CHUNK * (c % 2)
                rows = slice(r0, r0 + CHUNK)
                for g in range(2):
                    if c == 0:
                        dve.wait_ge(sem(f"delta_vector{g}"), DELTA_VECTOR[-1])
                        ins = V.tensor_copy(v_new[rows, g, :], u_sb[rows, g, :])
                    else:
                        dve.wait_ge(sem("state_used"), 2 * (c - 1) + g + 1)
                        ins = V.tensor_tensor(v_new[rows, g, :], u_sb[rows, g, :], bank[4 + 2 * g][rows, 0:S], ALU.subtract)
                    ins.then_inc(sem("v_new_ready"), 1)

            def state_and_output(c):
                t, r0 = c // 2, CHUNK * (c % 2)
                rows = slice(r0, r0 + CHUNK)

                def four(x):
                    return x.rearrange("p (m c) -> p m c", c=HD)

                for g in range(2):
                    own = slice(HD * g, HD * g + HD)
                    dve.wait_ge(sem("v_new_used"), 2 * c + g + 1)
                    if c < 3:
                        x, fresh = four(state[own, 0:S]), four(bank[5 + 2 * g][own, S:512])
                        if c == 0:
                            ins = V.tensor_copy(x, fresh)
                        else:
                            last = spread(exp_g[own, 16 + 4 * (c % 2):20 + 4 * (c % 2)], HD)
                            link(V.tensor_tensor(x, x, last, ALU.mult))
                            ins = V.tensor_tensor(x, x, fresh, ALU.add)
                        ins.then_inc(sem("state_ready"), 1)
                for g in range(2):
                    o = tok3[rows, t, 0:512].rearrange("p (m two c) -> p m two c", two=2, c=HD)[:, :, g, :]
                    inside = four(bank[5 + 2 * g][rows, 0:S])
                    if c == 0:
                        ins = V.tensor_copy(o, inside)
                    else:
                        tmp = four(o_tmp[rows, g, :])
                        link(V.tensor_tensor(tmp, four(bank[4 + 2 * g][rows, S:512]), spread(exp_g[rows, g:8:2], HD),
                                             ALU.mult))
                        ins = V.tensor_tensor(o, inside, tmp, ALU.add)
                    ins.then_inc(sem("o_stored"), 1)

            for kind, n, *stage in DELTA_SLOTS:
                if kind == "begin":
                    delta_begin(n)
                    if n == 0:
                        for g in range(2):
                            for c in range(2):
                                V.memset(diagonal[g][c * CHUNK:(c + 1) * CHUNK, :, (1 - c) * CHUNK:(2 - c) * CHUNK], 0.0)\
                                    .then_inc(sem("zeros_ready"), 1)
                        dve.wait_ge(sem("zeros_ready"), 4)
                elif kind == "stage":
                    for g in range(2):
                        delta_stage(n, *stage, g)
                elif kind == "old":
                    values(n)
                else:
                    if n == 0:
                        values(0)
                    state_and_output(n)

            def project(i, f):
                u = 35 + 2 * i + f // 2
                dve.wait_ge(sem("quarter_done"), 4 * (B_PROJ + i) + f + 1)
                at = 8 * (1 - i) + 2 * f
                x = gates[:, at:at + 2, :]
                V.scalar_tensor_tensor(x, x, 1.0, pair(u)[f % 2][:, :].rearrange("p (f s) -> p f s", s=S),
                                       ALU.add, ALU.mult).then_inc(sem(f"pair_free{u % 2}"), 1)
                if i:
                    dve.wait_ge(sem(f"pair_free{u % 2}"), 2 * (u // 2) + f % 2 + 1)
                    V.tensor_tensor(x, x, gates[:, 8 + 2 * f:10 + 2 * f, :], ALU.add).then_inc(sem("merged"), 1)

            dve.wait_ge(sem("o_stored"), 8)
            sq_o = o_squares.rearrange("p (t n) -> p t n", t=NT)
            for t in range(NT):
                ins = V.tensor_tensor(sq_o[:, t, :], tok3[:, t, 0:512], tok3[:, t, 0:512], ALU.mult)
            link(ins)
            link(V.tensor_reduce(stat[:, 64:80], o_squares.rearrange("p (g c) -> p g c", c=HD), AX_X, ALU.add))
            link(V.tensor_scalar(stat[:, 64:80], stat[:, 64:80], 1.0 / HD, RMS_EPS, ALU.mult, ALU.add))
            rsqrt(stat[:, 80:96], stat[:, 64:80], stat[:, 96:112])
            for t in range(NT):
                o = tok3[:, t, 0:512].rearrange("p (h c) -> p h c", c=HD)
                ins = V.tensor_tensor(o, o, spread(stat[:, 80 + 8 * t:88 + 8 * t], HD), ALU.mult)
            link(ins)
            for t in range(NT):
                V.scalar_tensor_tensor(tok3[:, t, 0:512], tok3[:, t, 0:512], 0.5, az[:, t, :], ALU.mult, ALU.mult)\
                    .then_inc(sem("o_gated"), 1)
            for k in range(4):
                mix_lo(k, 12 + k, v("a_norm"))
            for i in range(2):
                for f in range(4):
                    project(i, f)
            for f in range(4):
                dve.wait_ge(sem("merged_hi_done"), f + 1)
                V.scalar_tensor_tensor(h_lo[:, 2 * f:2 * f + 2, :], gates[:, 2 * f:2 * f + 2, :], 0.5,
                                       h_hi[:, 2 * f:2 * f + 2, :].bitcast(F32), ALU.mult, ALU.subtract)\
                    .then_inc(sem("merged_lo_done"), 1)
            for c in range(2):
                add_pair(4 * B_WOUT2 + WOUT2_ORDER.index((c, 3)) + 1, 39 + c, c)
            dve.wait_ge(sem("pair_free1"), 40)
            dve.wait_ge(sem("pair_free0"), 42)
            norm(4)
            norm_lo(4, "norm2")

            dve.wait_ge(sem("logits_ready"), 1)
            link(V.tensor_tensor(logits, bank[4][:, 0:NT * 20].rearrange("p (t n) -> p t n", t=NT),
                                 each_of(row[:, ROW["router_b"]], NT), ALU.add))
            glog, elog = logits[:, :, 0:4], logits[:, :, 4:20]
            prior = con[:, CON["prior"]]
            link(V.tensor_reduce(group_max, glog, AX_X, ALU.max))
            V.tensor_tensor(group_exp, glog, spread(group_max, 4), ALU.subtract).then_inc(sem("group_in_ready"), 1)

            def first_best(one, x, largest):
                n = x.shape[2]
                k = keys[:, :, 0:n]
                link(V.tensor_reduce(largest, x, AX_X, ALU.max))
                link(V.tensor_tensor(k, x, spread(largest, n), ALU.is_equal))
                link(V.tensor_tensor(k, k, each_of(prior[:, 0:n], NT), ALU.mult))
                link(V.tensor_reduce(best_key, k, AX_X, ALU.max))
                link(V.tensor_tensor(one, k, spread(best_key, n), ALU.is_equal))

            first_best(group_one, glog, top)
            link(V.tensor_scalar(group_one, group_one, -1.0, BIG, ALU.add, ALU.mult))
            for t in range(NT):
                ins = V.tensor_tensor(masked[:, t, :].rearrange("p (g e) -> p g e", e=4),
                                      elog[:, t, :].rearrange("p (g e) -> p g e", e=4), spread(group_one[:, t, :], 4), ALU.add)
            link(ins)
            first_best(first, masked, top)
            link(V.scalar_tensor_tensor(masked, first, -10 * BIG, masked, ALU.mult, ALU.add))
            first_best(second, masked, top2)
            V.tensor_tensor(second_exp, top2, top, ALU.subtract).then_inc(sem("second_in_ready"), 1)
            dve.wait_ge(sem("group_exp"), 1)
            link(V.tensor_reduce(group_sum, group_exp, AX_X, ALU.add))
            dve.wait_ge(sem("second_exp"), 1)
            link(V.scalar_tensor_tensor(w_first, second_exp, 1.0, group_sum, ALU.add, ALU.mult))
            link(V.reciprocal(w_first, w_first))
            link(V.tensor_tensor(w_second, second_exp, w_first, ALU.mult))
            link(V.tensor_tensor(first, first, spread(w_first, N_EXPERTS), ALU.mult))
            for t in range(NT):
                V.scalar_tensor_tensor(comb[:, t, :], second[:, t, :], w_second[:, t:t + 1], first[:, t, :],
                                       ALU.mult, ALU.add).then_inc(sem("comb_ready"), 1)

            def expert_product(b, i, n):
                dve.wait_ge(sem(f"pair_free{1 - i}"), n + (41 + i))
                dve.wait_ge(sem("quarter_done"), b + 4)
                V.tensor_tensor(e_act[:, i, :], e_act[:, i, :], pair_u[i][1][:, :], ALU.mult)\
                    .then_inc(sem(f"pair_free{1 - i}"), 1)

            def expert_weight(i, n):
                dve.wait_ge(sem(f"pair_free{1 - i}"), n + (42 + i))
                x = e_act[:, i, :].rearrange("p (f s) -> p f s", s=S)
                V.tensor_tensor(x, x, each_of(combs[:, bass.ds(n * S, S)], 2), ALU.mult)\
                    .then_inc(sem("expert_act_ready"), 1)

            def expert_lo(i, n):
                dve.wait_ge(sem("expert_hi_done"), n + 1)
                V.tensor_tensor(g_lo[:, 2 * i:2 * i + 2, :], e_act[:, i, :].rearrange("p (f s) -> p f s", s=S),
                                g_hi[:, 2 * i:2 * i + 2, :].bitcast(F32), ALU.subtract).then_inc(sem("expert_lo_done"), 1)

            b = 4 * B_MOE
            for i in range(2):
                expert_product(b + 4 * i, i, i)
            dve.wait_ge(sem("comb_turned"), 1)
            V.tensor_copy(comb_t, bank[4][0:N_EXPERTS, 0:S]).then_inc(sem("comb_t_stored"), 1)
            for e in range(0, N_EXPERTS, 2):
                dve.wait_ge(sem("comb_spread"), e // 2 + 1)
                V.tensor_copy(combs[:, e * S:(e + 2) * S], bank[5 + e // 2 % 3][:, :]).then_inc(sem("comb_stored"), 1)
            dve.wait_ge(sem("comb_stored"), N_EXPERTS // 2)
            for i in range(2):
                expert_weight(i, i)
            for i in range(2):
                expert_lo(i, i)

            def expert_step(b, n):
                for i in range(2):
                    expert_product(b + 4 * i, i, n + i)
                    expert_weight(i, n + i)
                    expert_lo(i, n + i)

            with dve.Fori(1, MOE_STEPS - 1) as i:
                expert_step(i * 12 + b, i * 2)
            expert_step(b + 12 * (MOE_STEPS - 1), 2 * (MOE_STEPS - 1))
            for t in range(NT):
                for c in range(2):
                    dve.wait_ge(sem("quarter_done"), N_QUARTERS)
                    part = x3[:, t, c * 512:(c + 1) * 512]
                    V.tensor_tensor(part, bank[4 + 2 * t + c][:, :], part, ALU.add).then_inc(sem("x_summed"), 1)
            dve.wait_ge(sem("x_summed"), 8)
            norm()
            dve.wait_ge(sem("norm_row2_loaded"), 16)
            for t in range(NT):
                V.scalar_tensor_tensor(tok3[:, t, :], x3[:, t, :], stat[:, 4 + t:5 + t], norm_row2, ALU.mult, ALU.mult)\
                    .then_inc(sem("final_ready"), 1)


def kernel(**a):
    from concourse import bacc
    from concourse.bass_utils import run_bass_kernel_spmd

    a = {name: np.asarray(value) for name, value in a.items()}
    weights, smalls = weight_stream(a)
    sel = np.zeros((N_EXPERTS, N_EXPERTS, P), np.float32)
    sel[np.arange(N_EXPERTS), np.arange(N_EXPERTS)] = 1.0
    arrays = {
        "weights": weights,
        "smalls": smalls,
        "x": np.ascontiguousarray(a["x"][0]),
        "p": np.ascontiguousarray(a["p"][0, 0].T.reshape(PLE_CHUNKS, P, S).transpose(1, 0, 2).reshape(P, -1)),
        "vectors": vector_columns(a),
        "constants": shape_constants(),
        "selectors": sel.reshape(N_EXPERTS, -1),
        "positions": np.ascontiguousarray(a["positions_2"][0]),
        "final_norm": np.ascontiguousarray(a["final_norm"]),
        "final_norm_2": np.ascontiguousarray(a["final_norm_g_2"]),
        "router_b": np.concatenate([a["b_router_group_2"][0], a["b_router_expert_2"][0]]),
        "a_log": np.ascontiguousarray(a["a_log_2"][0]),
        "dt_bias": np.ascontiguousarray(a["dt_bias_2"][0]),
    }
    nc = bacc.Bacc("TRN2", target_bir_lowering=False, num_devices=1)
    ap = {name: nc.dram_tensor(f"{name}_dram", v.shape, mybir.dt.from_np(v.dtype), kind="ExternalInput").ap()
          for name, v in arrays.items()}
    out = nc.dram_tensor("out_dram", (S, D), F32, kind="ExternalOutput").ap()
    rows = {name: ap[name] for name in ("final_norm", "final_norm_2", "router_b", "a_log", "dt_bias")}
    program(nc, ap["weights"], ap["smalls"], ap["x"], ap["p"], ap["vectors"], rows, ap["constants"], ap["selectors"],
            ap["positions"], out)
    r = run_bass_kernel_spmd(nc, [{f"{name}_dram": v for name, v in arrays.items()}], core_ids=[0])
    return r.results[0]["out_dram"].reshape(1, S, D)
```
